# Optimizing a Trainium2 kernel written in Bass

```python
import math
import numpy as np
import jax
import jax.numpy as jnp
from jax import lax

D_MODEL = 1024
BATCH = 1
SEQ = 256
DEPTH = 1

GDN_HEADS = 8
GDN_DK = 128
GDN_DV = 128
GDN_CONV = 4
GDN_CHUNK = 64
NSA_HEADS = 8
NSA_GROUPS = 2
NSA_DH = 128
CMP_BLOCK = 32
CMP_STRIDE = 16
CMP_HIDDEN = 256
SEL_BLOCK = 64
SEL_TOPN = 16
WINDOW = 512
NSA_Q_BLOCK = 32
FORCE_BONUS = 1000.0
REL_BUCKETS = 32
REL_MAX_DIST = 1024
FFN_HIDDEN = ((8 * D_MODEL + 3 * 256 - 1) // (3 * 256)) * 256
NORM_EPS = 1e-6

GDN_QK_W = GDN_HEADS * GDN_DK
GDN_V_W = GDN_HEADS * GDN_DV
NSA_W = NSA_HEADS * NSA_DH
NSA_KV_W = NSA_GROUPS * NSA_DH
IN_SPLITS = (GDN_QK_W, GDN_QK_W, GDN_V_W, GDN_V_W, GDN_HEADS, GDN_HEADS,
             NSA_W, 6 * NSA_KV_W, 3 * NSA_HEADS, 2 * D_MODEL)
IN_WIDTH = sum(IN_SPLITS)

kernel_name = "hybrid_gdn_nsa_gated_merge_swiglu"

def rmsnorm(x, w):
    xf = x.astype(jnp.float32)
    y = xf * lax.rsqrt(jnp.mean(xf * xf, axis=-1, keepdims=True) + NORM_EPS)
    return y.astype(x.dtype) * w

def l2norm(x):
    xf = x.astype(jnp.float32)
    return (xf * lax.rsqrt(jnp.sum(xf * xf, axis=-1, keepdims=True) + NORM_EPS)).astype(x.dtype)

def masked_softmax(logits, mask):
    s = jnp.where(mask, logits, -1e30)
    m = jnp.max(s, axis=-1, keepdims=True)
    p = jnp.where(mask, jnp.exp(s - m), 0.0)
    return p / jnp.maximum(jnp.sum(p, axis=-1, keepdims=True), 1e-30)

def rel_bucket(dist):
    dist = jnp.maximum(dist, 0)
    max_exact = REL_BUCKETS // 2
    d_f = jnp.maximum(dist, 1).astype(jnp.float32)
    large = max_exact + (jnp.log(d_f / max_exact) / math.log(REL_MAX_DIST / max_exact)
                         * (REL_BUCKETS - max_exact)).astype(jnp.int32)
    large = jnp.minimum(large, REL_BUCKETS - 1)
    return jnp.where(dist < max_exact, dist, large)

def causal_conv(x, w):
    c = x.shape[-1]
    return lax.conv_general_dilated(x, w[:, None, :], window_strides=(1,), padding=[(GDN_CONV - 1, 0)],
                                    dimension_numbers=("NWC", "WIO", "NWC"), feature_group_count=c)

def gdn_chunked(q, k, v, g, beta):
    b_, s_, h, dk = q.shape
    dv = v.shape[-1]
    c = GDN_CHUNK
    nc = s_ // c
    f32 = jnp.float32

    def chunks(t):
        return t.astype(f32).reshape(b_, nc, c, h, -1).transpose(0, 3, 1, 2, 4)

    qc, kc, vc = chunks(q), chunks(k), chunks(v)
    gc = g.astype(f32).reshape(b_, nc, c, h).transpose(0, 3, 1, 2)
    bc = beta.astype(f32).reshape(b_, nc, c, h).transpose(0, 3, 1, 2)
    gcum = jnp.cumsum(gc, axis=-1)
    idx = jnp.arange(c)
    tril = idx[:, None] >= idx[None, :]
    strict = idx[:, None] > idx[None, :]
    diff = gcum[..., :, None] - gcum[..., None, :]
    decay = jnp.where(tril, jnp.exp(jnp.where(tril, diff, 0.0)), 0.0)
    kb = kc * bc[..., None]
    vb = vc * bc[..., None]
    a_mat = jnp.where(strict, jnp.einsum("bhnid,bhnjd->bhnij", kb, kc) * decay, 0.0)
    rhs = jnp.concatenate([vb, kb * jnp.exp(gcum)[..., None]], axis=-1)
    sol = lax.linalg.triangular_solve(a_mat + jnp.eye(c, dtype=f32), rhs, left_side=True,
                                      lower=True, unit_diagonal=True)
    value, kcd = sol[..., :dv], sol[..., dv:]
    intra = jnp.einsum("bhnid,bhnjd->bhnij", qc, kc) * decay
    qg = qc * jnp.exp(gcum)[..., None]
    kdec = kc * jnp.exp(gcum[..., -1:] - gcum)[..., None]
    chunk_decay = jnp.exp(gcum[..., -1])
    xs = tuple(jnp.moveaxis(t, 2, 0) for t in (value, kcd, intra, qg, kdec, chunk_decay))

    def step(state, inp):
        val, kcd_n, intra_n, qg_n, kdec_n, cd_n = inp
        v_new = val - jnp.einsum("bhcd,bhde->bhce", kcd_n, state)
        o = jnp.einsum("bhcd,bhde->bhce", qg_n, state) + jnp.einsum("bhij,bhje->bhie", intra_n, v_new)
        state = state * cd_n[..., None, None] + jnp.einsum("bhcd,bhce->bhde", kdec_n, v_new)
        return state, o

    s0 = jnp.zeros((b_, h, dk, dv), f32)
    _, o = lax.scan(step, s0, xs)
    return o.transpose(1, 0, 3, 2, 4).reshape(b_, s_, h, dv).astype(v.dtype)

def compress(raw, pe, w1, w2):
    b_, s_, g, dh = raw.shape
    ratio = CMP_BLOCK // CMP_STRIDE
    nchunk = s_ // CMP_STRIDE
    ncmp = nchunk - ratio + 1
    ch = raw.reshape(b_, nchunk, CMP_STRIDE, g, dh)
    blocks = jnp.concatenate([ch[:, r:r + ncmp] for r in range(ratio)], axis=2)
    blocks = blocks + pe[None, None, :, None, :]
    flat = blocks.transpose(0, 1, 3, 2, 4).reshape(b_, ncmp, g, CMP_BLOCK * dh)
    return jax.nn.silu(flat @ w1) @ w2

def gated_deltanet(q_in, k_in, v_in, z, a, b, conv_w, a_log, dt_bias, gdn_norm_w):
    b_, s_, _ = q_in.shape
    qkv = jax.nn.silu(causal_conv(jnp.concatenate([q_in, k_in, v_in], axis=-1), conv_w))
    q, k, v = jnp.split(qkv, [GDN_QK_W, 2 * GDN_QK_W], axis=-1)
    q = l2norm(q.reshape(b_, s_, GDN_HEADS, GDN_DK)) * (GDN_DK ** -0.5)
    k = l2norm(k.reshape(b_, s_, GDN_HEADS, GDN_DK))
    v = v.reshape(b_, s_, GDN_HEADS, GDN_DV)
    g = -jnp.exp(a_log.astype(jnp.float32)) * jax.nn.softplus(a.astype(jnp.float32) + dt_bias.astype(jnp.float32))
    beta = jax.nn.sigmoid(b.astype(jnp.float32))
    o = gdn_chunked(q, k, v, g, beta)
    o = rmsnorm(o, gdn_norm_w) * jax.nn.silu(z.reshape(b_, s_, GDN_HEADS, GDN_DV))
    return o.reshape(b_, s_, GDN_V_W)

def native_sparse_attention(q_in, kv_in, gate_in, cmp_pe, cmp_w1, cmp_w2, q_norm_w, k_norm_w, rel_bias):
    b_, s_, _ = q_in.shape
    g_, r_, dh = NSA_GROUPS, NSA_HEADS // NSA_GROUPS, NSA_DH
    qb_sz = NSA_Q_BLOCK
    scale = dh ** -0.5
    q = rmsnorm(q_in.reshape(b_, s_, NSA_HEADS, dh), q_norm_w)
    kc_raw, vc_raw, ks, vs, kw, vw = [t.reshape(b_, s_, g_, dh) for t in jnp.split(kv_in, 6, axis=-1)]
    gates = jax.nn.sigmoid(gate_in).reshape(b_, s_, NSA_HEADS, 3)

    kc = rmsnorm(compress(kc_raw, cmp_pe[0], cmp_w1[0], cmp_w2[0]), k_norm_w[0])
    vc = compress(vc_raw, cmp_pe[1], cmp_w1[1], cmp_w2[1])
    ks = rmsnorm(ks, k_norm_w[1])
    kw = rmsnorm(kw, k_norm_w[2])

    ncmp = kc.shape[1]
    nsel = s_ // SEL_BLOCK
    topn = min(SEL_TOPN, nsel)
    cmp_start = jnp.arange(ncmp) * CMP_STRIDE
    cmp_end = cmp_start + CMP_BLOCK - 1
    sel_start = jnp.arange(nsel) * SEL_BLOCK
    overlap = ((cmp_start[:, None] < sel_start[None, :] + SEL_BLOCK)
               & (cmp_start[:, None] + CMP_BLOCK > sel_start[None, :])).astype(jnp.float32)
    ks_blk = ks.reshape(b_, nsel, SEL_BLOCK, g_, dh).transpose(0, 3, 1, 2, 4)
    vs_blk = vs.reshape(b_, nsel, SEL_BLOCK, g_, dh).transpose(0, 3, 1, 2, 4)
    kw_pad = jnp.pad(kw, ((0, 0), (WINDOW, 0), (0, 0), (0, 0)))
    vw_pad = jnp.pad(vw, ((0, 0), (WINDOW, 0), (0, 0), (0, 0)))
    table_gr = rel_bias.reshape(REL_BUCKETS, g_, r_)
    bi = jnp.arange(b_)[:, None, None, None]
    gi = jnp.arange(g_)[None, :, None, None]
    jsel = jnp.arange(nsel)

    def head_bias(dist):
        return rel_bias[rel_bucket(dist)].transpose(2, 0, 1).reshape(g_, r_, *dist.shape).astype(jnp.float32)

    def block(qs):
        t = qs + jnp.arange(qb_sz)
        qb = lax.dynamic_slice_in_dim(q, qs, qb_sz, axis=1).reshape(b_, qb_sz, g_, r_, dh)
        gb = lax.dynamic_slice_in_dim(gates, qs, qb_sz, axis=1).reshape(b_, qb_sz, g_, r_, 3)
        lc = jnp.einsum("bqgrd,bngd->bgrqn", qb, kc).astype(jnp.float32) * scale \
            + head_bias(t[:, None] - cmp_end[None, :])
        pc = masked_softmax(lc, cmp_end[None, :] <= t[:, None])
        oc = jnp.einsum("bgrqn,bngd->bqgrd", pc.astype(vc.dtype), vc)
        imp = jnp.einsum("bgrqn,nj->bgqj", pc, overlap)
        tb = t // SEL_BLOCK
        forced = (jsel[None, :] == 0) | (jsel[None, :] == tb[:, None]) | (jsel[None, :] == tb[:, None] - 1)
        score = jnp.where(jsel[None, :] <= tb[:, None], imp + FORCE_BONUS * forced, -1e30)
        _, idx = lax.top_k(score, topn)
        k_sel = ks_blk[bi, gi, idx]
        v_sel = vs_blk[bi, gi, idx]
        pos = idx[..., None] * SEL_BLOCK + jnp.arange(SEL_BLOCK)
        dist = t[None, None, :, None, None] - pos
        bias_s = table_gr[rel_bucket(dist), gi[..., None]].transpose(0, 1, 5, 2, 3, 4).astype(jnp.float32)
        ls = jnp.einsum("bqgrd,bgqnkd->bgrqnk", qb, k_sel).astype(jnp.float32) * scale + bias_s
        ls = ls.reshape(b_, g_, r_, qb_sz, topn * SEL_BLOCK)
        ms = (dist >= 0).reshape(b_, g_, 1, qb_sz, topn * SEL_BLOCK)
        ps = masked_softmax(ls, ms)
        o_s = jnp.einsum("bgrqm,bgqmd->bqgrd", ps.astype(v_sel.dtype),
                         v_sel.reshape(b_, g_, qb_sz, topn * SEL_BLOCK, dh))
        kwin = lax.dynamic_slice_in_dim(kw_pad, qs, WINDOW + qb_sz, axis=1)
        vwin = lax.dynamic_slice_in_dim(vw_pad, qs, WINDOW + qb_sz, axis=1)
        wpos = qs - WINDOW + jnp.arange(WINDOW + qb_sz)
        wd = t[:, None] - wpos[None, :]
        lw = jnp.einsum("bqgrd,bkgd->bgrqk", qb, kwin).astype(jnp.float32) * scale + head_bias(wd)
        pw = masked_softmax(lw, (wd >= 0) & (wd < WINDOW) & (wpos[None, :] >= 0))
        ow = jnp.einsum("bgrqk,bkgd->bqgrd", pw.astype(vwin.dtype), vwin)
        o = gb[..., 0:1] * oc + gb[..., 1:2] * o_s + gb[..., 2:3] * ow
        return o.reshape(b_, qb_sz, NSA_W)

    out = lax.map(block, jnp.arange(s_ // qb_sz) * qb_sz)
    return out.transpose(1, 0, 2, 3).reshape(b_, s_, NSA_W)

def setup_inputs(seed: int = 0) -> dict:
    key = jax.random.key(seed)
    ks = jax.random.split(key, 21)
    L = DEPTH
    f32 = jnp.float32

    def nrm(k, shape, scale):
        return jax.random.normal(k, shape, f32) * scale

    dt = jnp.exp(jax.random.uniform(ks[5], (L, GDN_HEADS), f32, math.log(1e-3), math.log(1e-1)))
    return {
        "x": nrm(ks[0], (BATCH, SEQ, D_MODEL), 1.0),
        "norm1_w": 1.0 + nrm(ks[1], (L, D_MODEL), 0.02),
        "w_in": nrm(ks[2], (L, D_MODEL, IN_WIDTH), D_MODEL ** -0.5),
        "conv_w": nrm(ks[3], (L, GDN_CONV, 2 * GDN_QK_W + GDN_V_W), GDN_CONV ** -0.5),
        "a_log": jnp.log(jax.random.uniform(ks[4], (L, GDN_HEADS), f32, 1.0, 16.0)),
        "dt_bias": dt + jnp.log(-jnp.expm1(-dt)),
        "gdn_norm_w": 1.0 + nrm(ks[6], (L, GDN_DV), 0.02),
        "cmp_pe": nrm(ks[7], (L, 2, CMP_BLOCK, NSA_DH), 0.02),
        "cmp_w1": nrm(ks[8], (L, 2, CMP_BLOCK * NSA_DH, CMP_HIDDEN), (CMP_BLOCK * NSA_DH) ** -0.5),
        "cmp_w2": nrm(ks[9], (L, 2, CMP_HIDDEN, NSA_DH), CMP_HIDDEN ** -0.5),
        "q_norm_w": 1.0 + nrm(ks[10], (L, NSA_DH), 0.02),
        "k_norm_w": 1.0 + nrm(ks[11], (L, 3, NSA_DH), 0.02),
        "rel_bias": nrm(ks[12], (REL_BUCKETS, NSA_HEADS), 0.5),
        "w_proj_a": nrm(ks[13], (L, GDN_V_W, D_MODEL), GDN_V_W ** -0.5),
        "w_proj_b": nrm(ks[14], (L, NSA_W, D_MODEL), NSA_W ** -0.5),
        "w_out": nrm(ks[15], (L, D_MODEL, D_MODEL), D_MODEL ** -0.5),
        "norm2_w": 1.0 + nrm(ks[16], (L, D_MODEL), 0.02),
        "w_gate": nrm(ks[17], (L, D_MODEL, FFN_HIDDEN), D_MODEL ** -0.5),
        "w_up": nrm(ks[18], (L, D_MODEL, FFN_HIDDEN), D_MODEL ** -0.5),
        "w_down": nrm(ks[19], (L, FFN_HIDDEN, D_MODEL), FFN_HIDDEN ** -0.5),
    }

def reference(x, norm1_w, w_in, conv_w, a_log, dt_bias, gdn_norm_w, cmp_pe, cmp_w1, cmp_w2,
              q_norm_w, k_norm_w, rel_bias, w_proj_a, w_proj_b, w_out, norm2_w, w_gate, w_up, w_down):
    offsets = [int(o) for o in np.cumsum(IN_SPLITS)[:-1]]
    for l in range(DEPTH):
        h = rmsnorm(x, norm1_w[l])
        proj = h @ w_in[l]
        (gq, gk, gv, gz, ga, gb, nq, nkv, ngate, mgate) = jnp.split(proj, offsets, axis=-1)
        y_a = gated_deltanet(gq, gk, gv, gz, ga, gb, conv_w[l], a_log[l], dt_bias[l], gdn_norm_w[l])
        y_b = native_sparse_attention(nq, nkv, ngate, cmp_pe[l], cmp_w1[l], cmp_w2[l],
                                      q_norm_w[l], k_norm_w[l], rel_bias)
        gate_a, gate_b = jnp.split(jax.nn.sigmoid(mgate), 2, axis=-1)
        mixed = gate_a * (y_a @ w_proj_a[l]) + gate_b * (y_b @ w_proj_b[l])
        x = x + mixed @ w_out[l]
        h2 = rmsnorm(x, norm2_w[l])
        x = x + (jax.nn.silu(h2 @ w_gate[l]) * (h2 @ w_up[l])) @ w_down[l]
    return x


_drawn_inputs = setup_inputs


def setup_inputs(seed=0):
    import zlib

    import numpy as np

    out = dict(_drawn_inputs(seed))
    spreads = {}
    factors = {'norm1_w': 4.28,
     'gdn_norm_w': 8.0,
     'cmp_pe': 43.521,
     'q_norm_w': 8.0,
     'k_norm_w': 8.0,
     'norm2_w': 13.517,
     'rel_bias': 4.98}
    for name, (base, spread) in spreads.items():
        noise = np.random.default_rng([zlib.crc32(name.encode()), seed]).standard_normal(out[name].shape)
        drawn = base * np.exp(spread * noise) if base else spread * noise
        out[name] = jnp.asarray(drawn.astype(out[name].dtype))
    for name, factor in factors.items():
        out[name] = (out[name] * factor).astype(out[name].dtype)
    return out
```

```python
import math
from contextlib import ExitStack

import concourse.bass as bass
import numpy as np
from concourse import mybir

D_MODEL, SEQ = 1024, 256
HEADS, DH = 8, 128
GROUPS = 2
CMP_BLOCK, CMP_STRIDE, CMP_HIDDEN = 32, 16, 256
NCMP = SEQ // CMP_STRIDE - CMP_BLOCK // CMP_STRIDE + 1
CONV = 4
REL_BUCKETS, REL_MAX_DIST = 32, 1024
FFN = ((8 * D_MODEL + 3 * 256 - 1) // (3 * 256)) * 256
EPS = 1e-6
P = 128
TT = SEQ // P
KT = D_MODEL // P
CW = 256
LEVELS = int(math.log2(P))
NEG = -1e30

GQ, GK, GV, GZ = (i * D_MODEL for i in range(4))
GA = 4 * D_MODEL
NQ = GA + 2 * HEADS
NKV = NQ + D_MODEL
KV_W = GROUPS * DH
NGATE = NKV + 6 * KV_W
MGATE = NGATE + 3 * HEADS
NSMALL = 2 * HEADS + 3 * HEADS

ROW_N1, ROW_N2, ROW_GDN, ROW_QN, ROW_KN, ROW_PE = 0, KT, 2 * KT, 2 * KT + 1, 2 * KT + 2, 2 * KT + 5
NROWS = ROW_PE + 2 * CMP_BLOCK


def weight_chunks():
    out = [("gk", i) for i in range(4)] + [("gq", i) for i in range(4)] + [("gv", i) for i in range(4)]
    out += [("kc", 0), ("vc", 0)] + [("cmpk", i) for i in range(4)] + [("nq", i) for i in range(4)]
    out += [("ks", 0)] + [("cmpv", i) for i in range(4)] + [("vs", 0), ("kw", 0), ("vw", 0)] + [("gz", i) for i in range(4)]
    for i in range(4):
        out += [("mga", i), ("pa", i)]
    for i in range(4):
        out += [("mgb", i), ("pb", i)]
    out += [("wo", i) for i in range(4)]
    nf = FFN // P
    for j in range(nf // 2):
        out += [("gu", 2 * j), ("gu", 2 * j + 1)]
        if j >= 1:
            out += [("dn", j - 1)]
    out += [("dn", nf // 2 - 1)]
    return out


CHUNKS = weight_chunks()
AT = {k: n for n, k in enumerate(CHUNKS)}
TOKEN_MAJOR = ("ks", "vs", "kw", "vw", "wo")
NO_BANK = ("cmpk", "cmpv", "dn")
COPIED = ("gk", "gq", "gv", "nq", "ks", "vs", "kw", "vw", "kc", "vc")
BANK_USE, COPY_NO = {}, {}
for _n, (_k, _i) in enumerate(CHUNKS):
    if _k not in NO_BANK:
        BANK_USE[_n] = len(BANK_USE)
    if _k in COPIED:
        COPY_NO[_n] = len(COPY_NO)
BANK_USER = {u: n for n, u in BANK_USE.items()}

STAGES = ["row", "kt", "vt", "knT", "gram", "kq", "m1t", "at"]
for _l in range(1, LEVELS):
    STAGES += [f"X{_l}"] + ([f"Y{_l}"] if _l < LEVELS - 1 else []) + [f"Z{_l}"]
STAGES += ["w0", "s1", "v1", "o1", "ot"]
NB = 4
GRING = 3


def stage_use(name, b):
    return NB * STAGES.index(name) + b


FIRST_STAGE_SLOT = AT["gv", 3] + 1
UNITS = [(h, t) for h in range(HEADS) for t in range(TT)]
FIRST_UNIT_SLOT = AT["gz", 1]


def slot_stages(n, half):
    if (n, half) == (AT["mga", 0], 0):
        return ["ot"]
    i = 2 * (n - FIRST_STAGE_SLOT) + half
    return [STAGES[i]] if 0 <= i < len(STAGES) - 1 else []


W2_K, TURN_KC, LOGITS_C, W2_V, TURN_PC, TURN_KS, TURN_KW = 0, 1, 2, 3, 4, 8, 9
MISC_SLOTS = {W2_K: (AT["nq", 0], 1), TURN_KC: (AT["nq", 1], 1), LOGITS_C: (AT["cmpv", 1], 1), W2_V: (AT["vs", 0], 1),
              TURN_PC: (AT["kw", 0], 0), TURN_PC + 1: (AT["kw", 0], 1), TURN_PC + 2: (AT["vw", 0], 0), TURN_PC + 3: (AT["vw", 0], 1),
              TURN_KS: (AT["gz", 0], 0), TURN_KW: (AT["gz", 0], 1)}


def slot_misc(n, half):
    return [m for m, where in MISC_SLOTS.items() if where == (n, half)]


def slot_units(n, half):
    i = 2 * (n - FIRST_UNIT_SLOT) + half
    return [i] if 0 <= i < len(UNITS) + 2 else []


def hybrid_block(nc, x, norm1_w, w_in, conv_w, a_log, dt_bias, gdn_norm_w, cmp_pe, cmp_w1, cmp_w2,
                 q_norm_w, k_norm_w, rel_bias, w_proj_a, w_proj_b, w_out, norm2_w, w_gate, w_up, w_down,
                 c_ident, c_upper, c_negmask, c_levels, c_onehot, c_rowvalid, c_flip, bias_rows, out):
    f32, f32r, i32, u8 = mybir.dt.float32, mybir.dt.float32r, mybir.dt.int32, mybir.dt.uint8
    ALU, ACT, AX = mybir.AluOpType, mybir.ActivationFunctionType, mybir.AxisListType
    ctx = ExitStack()
    with ctx:
        KB = 1024
        base = 16512
        cursor = [base]

        def at(name, addr, shape, dt=f32):
            return nc.alloc_sbuf_tensor_at(name, shape, dt, offset=addr)

        def take(nbytes):
            a = cursor[0]
            cursor[0] += (nbytes + 31) // 32 * 32
            return a

        def own(name, shape, dt=f32):
            n = int(np.prod(shape[1:])) * (1 if dt == u8 else 4)
            return at(name, take(n), shape, dt)

        NRAW, NSPL = 3, 2
        raw = [own(f"raw{i}", [P, KT, CW]) for i in range(NRAW)]
        w_hi = [own(f"w_hi{i}", [P, KT, CW], f32r) for i in range(NSPL)]
        w_lo = [own(f"w_lo{i}", [P, KT, CW], f32r) for i in range(NSPL)]
        h_hi, h_lo = own("h_hi", [P, KT, SEQ], f32r), own("h_lo", [P, KT, SEQ], f32r)
        yb_at = take(16 * KB)
        yb_hi, yb_lo = at("yb_hi", yb_at, [P, KT, SEQ], f32r), at("yb_lo", yb_at + 8 * KB, [P, KT, SEQ], f32r)
        cmp_raw = at("cmp_raw", yb_at, [P, 2, GROUPS, SEQ])
        flat_hi = at("flat_hi", yb_at + 4 * KB, [P, CMP_BLOCK, 32], f32r)
        flat_lo = at("flat_lo", yb_at + 8 * KB, [P, CMP_BLOCK, 32], f32r)
        key_tok = at("key_tok", yb_at + 12 * KB, [P, 2, 4, DH])
        pcT = at("pcT", yb_at, [NCMP, 16, P])
        arena = take(72 * KB)

        def ar(i, name, shape=(P, 16, P), dt=f32, off=0):
            return at(name, arena + i * 8 * KB + off, list(shape), dt)

        kT, qT, vT, kn, ET, AXb, ATb, Db, DTb = (ar(i, n) for i, n in enumerate(
            ["kT", "qT", "vT", "kn", "ET", "AXb", "ATb", "Db", "DTb"]))
        x_sb = ar(0, "x_sb", (P, TT, D_MODEL))
        xn_sb = ar(1, "xn_sb", (P, TT, D_MODEL))
        cin = [ar(5, f"cin{i}", (P, 2, SEQ + 8), off=i * 2112) for i in range(2)]
        cacc = [ar(6, f"cacc{i}", (P, 2, SEQ), off=i * 2 * KB) for i in range(2)]
        cth = [ar(6, f"cth{i}", (P, 2, SEQ), off=(2 + i) * 2 * KB) for i in range(2)]
        csq = [ar(7, f"csq{i}", (P, 2, SEQ), off=i * 2 * KB) for i in range(2)]
        ya_hi, ya_lo = ar(5, "ya_hi", (P, KT, SEQ), f32r), ar(6, "ya_lo", (P, KT, SEQ), f32r)
        mix = ar(7, "mix", (P, KT, SEQ))
        mix_hi, mix_lo = ar(3, "mix_hi", (P, KT, SEQ), f32r), ar(4, "mix_lo", (P, KT, SEQ), f32r)
        x1 = ar(0, "x1", (P, TT, D_MODEL))
        x1n = ar(1, "x1n", (P, TT, D_MODEL))
        sg = [ar(2, f"sg{i}", (P, SEQ), off=i * KB) for i in range(2)]
        gu = [ar(2, f"gu{i}", (P, SEQ), off=(2 + i) * KB) for i in range(2)]
        g_hi = [ar(8, f"g_hi{i}", (P, SEQ), f32r, off=i * KB) for i in range(4)]
        g_lo = [ar(8, f"g_lo{i}", (P, SEQ), f32r, off=(4 + i) * KB) for i in range(4)]
        out_sb = ar(1, "out_sb", (P, TT, D_MODEL))
        pmix = ar(8, "pmix", (P, 2, SEQ))

        z_at = cursor[0]
        zsT = own("zsT", [P, HEADS, SEQ])
        cmp2 = at("cmp2", z_at, [P, 2, 2, DH])
        kc = at("kc", z_at + 2 * KB, [NCMP, GROUPS, DH])
        pc = at("pc", z_at + 3 * KB, [P, HEADS, TT, NCMP])
        pcm = at("pcm", z_at + 4 * KB, [P, HEADS, TT])
        pcs = at("pcs", z_at + 4 * KB + 64, [P, HEADS, TT])
        nqT = own("nqT", [P, HEADS, SEQ])
        bias_up = at("bias_up", cursor[0] - 8 * KB, [P, HEADS, SEQ])
        bias_g = own("bias_g", [P, HEADS, SEQ])
        ksT, kwT = own("ksT", [P, GROUPS, SEQ]), own("kwT", [P, GROUPS, SEQ])
        vs, vw = own("vs", [P, TT, GROUPS, DH]), own("vw", [P, TT, GROUPS, DH])
        sc_at = take(4 * KB)
        sc = [at(f"sc{i}", sc_at + i * 2 * KB, [P, 2, SEQ]) for i in range(2)]
        pt_at = take(4 * KB)
        pt = [at(f"pt{i}", pt_at + i * 2 * KB, [P, 4, P]) for i in range(2)]
        hid = at("hid", pt_at, [P, 2, 2, 32])
        rows_a = at("rows_a", sc_at, [CONV * 24, P])
        rows_b = at("rows_b", sc_at + 512, [NROWS, P])
        wsm = at("wsm", sc_at + KB, [P, KT, NSMALL])
        wsm_hi = at("wsm_hi", pt_at, [P, KT, NSMALL], f32r)
        wsm_lo = at("wsm_lo", pt_at + 1280, [P, KT, NSMALL], f32r)
        gate_t = own("gate_t", [P, 2, SEQ])
        nsq = at("nsq", cursor[0] - 2 * KB, [P, 2, SEQ])
        ident, upper, negmask = own("ident", [P, P]), own("upper", [P, P]), own("negmask", [P, P])
        vc = at("vc", cursor[0] - KB, [NCMP, GROUPS, DH])
        ones = own("ones", [P, 4])
        ones_sq = ar(8, "ones_sq", (P, P))
        cols_a = ar(8, "cols_a", (P, CONV * 24), off=512)
        flip = ar(8, "flip", (P, P), off=KB)
        levels = own("levels", [P, 2 * LEVELS, P], u8)
        onehot = at("onehot", sc_at + 2560, [REL_BUCKETS + 1, 384])
        relb = own("relb", [REL_BUCKETS + 1, HEADS])
        bias_v = at("bias_v", pt_at + 2560, [HEADS, 384])
        cols_b = own("cols_b", [P, NROWS])
        small = own("small", [P, TT, NSMALL])
        rowvalid = own("rowvalid", [P, 1])
        par = own("par", [P, 2, HEADS])
        col = {n: own("c_" + n, [P, HEADS, TT]) for n in (
            "g", "gc", "gl", "eg", "beta", "hbeta", "nbeta", "kf", "rk", "rq", "rn", "ss", "of", "t0", "t1", "t2")}
        gates = own("gates", [P, TT, 3 * HEADS])
        ksum = own("ksum", [P, 8])
        kr = own("kr", [P, 8])
        wk = own("wk", [P, 3])
        zw = own("zw", [P, 1])
        scol = {n: own("s_" + n, [P, 8]) for n in ("a", "b", "c", "d", "x", "nm", "se", "fac")}
        kcT = own("kcT", [P, GROUPS, 16])

        ps = [ctx.enter_context(nc.psum_tensor(f"ps{i}", [P, 512], f32)) for i in range(8)]
        stream_ps = ps[0:2]
        gdn_ps = ps[2:5]
        log_ps, pt_ps, pv_ps = ps[5], ps[6], ps[7]

        def sem(name):
            return ctx.enter_context(nc.semaphore(name))

        raw_in = [sem(f"raw_in{i}") for i in range(NRAW)]
        hi_done, lo_done = sem("hi_done"), sem("lo_done")
        half_done = sem("half_done")
        copied = sem("copied")
        x_in, vec_in, const_in, levels_in, small_in, misc_in = sem("x_in"), sem("vec_in"), sem("const_in"), sem("levels_in"), sem("small_in"), sem("misc_in")
        bias_out, bias_in, bias_mm, bias_done = sem("bias_out"), sem("bias_in"), sem("bias_mm"), sem("bias_done")
        flip_ps = [ps[2], ps[3], ps[4], ps[6]]
        xres_in, out_done = sem("xres_in"), sem("out_done")
        ones_set, relb_set, d_init = sem("ones_set"), sem("relb_set"), sem("d_init")
        dve_step, act_step, pool_step = sem("dve_step"), sem("act_step"), sem("pool_step")
        pre_pe, pre_dve, pre_act = sem("pre_pe"), sem("pre_dve"), sem("pre_act")
        xss, xn_done = sem("xss"), sem("xn_done")
        tr_ready, h_hi_done, h_lo_done = sem("tr_ready"), sem("h_hi_done"), sem("h_lo_done")
        conv_in, conv_acc, conv_th, conv_done, conv_sq, colsum = (sem(n) for n in (
            "conv_in", "conv_acc", "conv_th", "conv_done", "conv_sq", "colsum"))
        cols_ready, rk_ready, rq_ready, rn_ready = sem("cols_ready"), sem("rk_ready"), sem("rq_ready"), sem("rn_ready")
        g_mm = sem("g_mm")
        g_out = [sem(f"g_out{i}") for i in range(GRING)]
        et_ready, lvl0, kf_ready, ss_ready, on_ready = (sem(n) for n in (
            "et_ready", "lvl0", "kf_ready", "ss_ready", "on_ready"))
        o_ready, of_ready, zt, zs_done = sem("o_ready"), sem("of_ready"), sem("zt"), sem("zs_done")
        nq_in, nq_sq = sem("nq_in"), sem("nq_sq")
        key_in, key_rs, key_n = sem("key_in"), sem("key_rs"), sem("key_n")
        cmp_in, flat_done = sem("cmp_in"), sem("flat_done")
        m_pe, m_out = sem("m_pe"), sem("m_out")
        hid_th, hid_done, pc_s, pc_e = sem("hid_th"), sem("hid_done"), sem("pc_s"), sem("pc_e")
        l_mm, s_done, e_done, p_done, t_mm, t_out, v_mm, v_out = (sem(n) for n in (
            "l_mm", "s_done", "e_done", "p_done", "t_mm", "t_out", "v_mm", "v_out"))
        ya_hi_done, ya_lo_done, yb_hi_done, yb_lo_done = (sem(n) for n in ("ya_hi_done", "ya_lo_done", "yb_hi_done", "yb_lo_done"))
        mg_done, pa_done, pb_read, mix_done, mix_hi_done, mix_lo_done = (sem(n) for n in (
            "mg_done", "pa_done", "pb_read", "mix_done", "mix_hi_done", "mix_lo_done"))
        x1_done, sg_done, gu_done, g_hi_done, g_lo_done, fin = (sem(n) for n in (
            "x1_done", "sg_done", "gu_done", "g_hi_done", "g_lo_done", "fin"))

        def wait_bank(eng, n):
            if n not in BANK_USE or BANK_USE[n] < 2:
                return
            m = BANK_USER[BANK_USE[n] - 2]
            kind, i = CHUNKS[m]
            if kind in COPIED:
                eng.wait_ge(copied, COPY_NO[m] + 1)
            elif kind in ("mga", "mgb"):
                eng.wait_ge(mg_done, i + 1 + (4 if kind == "mgb" else 0))
            else:
                eng.wait_ge({"gz": zs_done, "pa": pa_done, "pb": pb_read, "wo": x1_done, "gu": gu_done}[kind], i + 1)

        def chunk_source(n):
            kind, i = CHUNKS[n]
            wide = lambda w, c: w.rearrange("(k p) n -> p k n", p=P)[:, :, c:c + CW]
            first = {"gk": GK, "gq": GQ, "gv": GV, "gz": GZ, "nq": NQ, "kc": NKV, "vc": NKV + KV_W, "ks": NKV + 2 * KV_W,
                     "vs": NKV + 3 * KV_W, "kw": NKV + 4 * KV_W, "vw": NKV + 5 * KV_W, "mga": MGATE, "mgb": MGATE + D_MODEL}
            if kind in first:
                return [(slice(0, CW), wide(w_in[0], first[kind] + i * CW))]
            if kind in ("pa", "pb", "wo"):
                return [(slice(0, CW), wide({"pa": w_proj_a, "pb": w_proj_b, "wo": w_out}[kind][0], i * CW))]
            if kind in ("cmpk", "cmpv"):
                w = cmp_w1[0, 0 if kind == "cmpk" else 1].rearrange("(j p) n -> p j n", p=P)
                return [(slice(0, CW), w[:, i * KT:(i + 1) * KT, :])]
            if kind == "gu":
                return [(slice(0, P), w_gate[0].rearrange("(k p) n -> p k n", p=P)[:, :, i * P:(i + 1) * P]),
                        (slice(P, CW), w_up[0].rearrange("(k p) n -> p k n", p=P)[:, :, i * P:(i + 1) * P])]
            return [(None, w_down[0].rearrange("(k p) n -> p k n", p=P)[:, 2 * i:2 * i + 2, :])]

        def loads_before(n):
            return sum(len(chunk_source(m)) for m in range(n % NRAW, n + 1, NRAW))

        def wait_use(eng, name, b):
            u = stage_use(name, b)
            eng.wait_ge(g_out[u % GRING], u // GRING + 1)

        def problems(t, b):
            return t[:, 4 * b:4 * b + 4, :]

        def pcol(name, b):
            return col[name][:, 2 * b:2 * b + 2, :].rearrange("p h t -> p (h t)")

        def wide_col(name, b):
            return pcol(name, b).unsqueeze(2).to_broadcast([P, 4, P])

        block = ctx.enter_context(nc.Block())

        @block.sync
        def _(sp):
            sp.dma_start(x_sb[:], x[0].rearrange("(t p) d -> p t d", p=P)).then_inc(x_in, 16)
            sp.dma_start(ident[:], c_ident).then_inc(const_in, 16)

            def load_chunk(n):
                if n >= NRAW:
                    sp.wait_ge(hi_done, n - NRAW + 1)
                    sp.wait_ge(lo_done, n - NRAW + 1)
                for where, src in chunk_source(n):
                    r = raw[n % NRAW]
                    dst = r[:, :, where] if where is not None else r[:].rearrange("p k c -> p (k c)").rearrange("p (k c) -> p k c", k=2)
                    sp.dma_start(dst, src).then_inc(raw_in[n % NRAW], 16)

            for n in range(NRAW):
                load_chunk(n)
            for n in range(NRAW, len(CHUNKS)):
                load_chunk(n)
            for i in range(4):
                sp.wait_ge(fin, i + 1)
                t, c = i // 2, i % 2
                sp.dma_start(out[0].rearrange("(t p) d -> p t d", p=P)[:, t, c * 512:(c + 1) * 512],
                             out_sb[:, t, c * 512:(c + 1) * 512]).then_inc(out_done, 16)
            sp.wait_ge(out_done, 64)

        @block.gpsimd
        def _(pool):
            nc.gpsimd.memset(ones[:], 1.0).then_inc(ones_set, 1)
            nc.gpsimd.memset(ones_sq[:], 1.0).then_inc(ones_set, 1)
            nc.gpsimd.memset(relb[:], 1.0).then_inc(relb_set, 1)
            pool.wait_ge(relb_set, 1)
            pool.dma_start(relb[0:REL_BUCKETS, :], rel_bias).then_inc(misc_in, 16)
            pool.dma_start(onehot[:], c_onehot).then_inc(misc_in, 16)
            pool.dma_start(cmp2[:], cmp_w2[0].rearrange("c (k p) d -> p c k d", p=P)).then_inc(misc_in, 16)
            pool.dma_start(rowvalid[:], c_rowvalid).then_inc(misc_in, 16)
            pool.dma_start(par[:, 0, :], a_log[0:1, :].to_broadcast([P, HEADS])).then_inc(misc_in, 16)
            pool.dma_start(par[:, 1, :], dt_bias[0:1, :].to_broadcast([P, HEADS])).then_inc(misc_in, 16)
            pool.dma_start(flip[:], c_flip).then_inc(bias_in, 16)
            pool.dma_start(levels[:], c_levels).then_inc(levels_in, 16)
            pool.wait_ge(pre_dve, 4)
            pool.dma_start(bias_rows, bias_v[:]).then_inc(bias_out, 16)
            pool.wait_ge(bias_out, 16)
            pool.dma_start(bias_up[:], bass.AP(bias_rows.tensor, 0, [[1, P], [384, HEADS], [1, SEQ]])).then_inc(bias_in, 16)
            pool.wait_ge(conv_done, 12)
            pool.wait_ge(colsum, 8)
            pool.wait_ge(const_in, 48)
            nc.gpsimd.tensor_copy(Db[:], ident[:].unsqueeze(1).to_broadcast([P, 16, P])).then_inc(d_init, 1)
            nc.gpsimd.tensor_copy(DTb[:], ident[:].unsqueeze(1).to_broadcast([P, 16, P])).then_inc(d_init, 1)
            for b in range(NB):
                pool.wait_ge(g_mm, stage_use("knT", b) + 1)
                nc.gpsimd.tensor_tensor(problems(kn, b), problems(kn, b), wide_col("kf", b), ALU.mult).then_inc(kf_ready, 1)
            for b in range(NB):
                pool.wait_ge(of_ready, b + 1)
                nc.gpsimd.tensor_tensor(problems(kT, b), problems(kT, b), wide_col("of", b), ALU.mult).then_inc(on_ready, 1)

        @block.scalar
        def _(act):
            count = [0]

            def link(ins):
                count[0] += 1
                ins.then_inc(act_step, 1)
                act.wait_ge(act_step, count[0])

            act.dma_start(upper[:], c_upper).then_inc(const_in, 16)
            act.dma_start(negmask[:], c_negmask).then_inc(const_in, 16)
            act.dma_start(rows_a[:], conv_w[0].rearrange("j (c p) -> (j c) p", p=P)).then_inc(vec_in, 16)
            act.dma_start(rows_b[ROW_N1:ROW_N1 + KT, :], norm1_w[0].rearrange("(k p) -> k p", p=P)).then_inc(vec_in, 16)
            act.dma_start(rows_b[ROW_N2:ROW_N2 + KT, :], norm2_w[0].rearrange("(k p) -> k p", p=P)).then_inc(vec_in, 16)
            act.dma_start(rows_b[ROW_GDN:ROW_GDN + 1, :], gdn_norm_w).then_inc(vec_in, 16)
            act.dma_start(rows_b[ROW_QN:ROW_QN + 1, :], q_norm_w).then_inc(vec_in, 16)
            act.dma_start(rows_b[ROW_KN:ROW_KN + 3, :], k_norm_w[0]).then_inc(vec_in, 16)
            act.dma_start(rows_b[ROW_PE:NROWS, :], cmp_pe[0].rearrange("c j d -> (c j) d")).then_inc(vec_in, 16)
            wi = w_in[0].rearrange("(k p) n -> p k n", p=P)
            act.dma_start(wsm[:, :, 0:2 * HEADS], wi[:, :, GA:GA + 2 * HEADS]).then_inc(small_in, 16)
            act.dma_start(wsm[:, :, 2 * HEADS:], wi[:, :, NGATE:NGATE + 3 * HEADS]).then_inc(small_in, 16)

            def split_hi(n):
                act.wait_ge(raw_in[n % NRAW], 16 * loads_before(n))
                if n >= NSPL:
                    act.wait_ge(half_done, 2 * (n - NSPL) + 2)
                nc.scalar.activation(w_hi[n % NSPL][:], raw[n % NRAW][:], ACT.Copy).then_inc(hi_done, 1)

            act.wait_ge(x_in, 16)
            for t in range(TT):
                nc.scalar.activation(xn_sb[:, t, :], x_sb[:, t, :], ACT.Square, accum_out=scol["x"][:, t:t + 1]).then_inc(xss, 1)
            split_hi(0)
            act.wait_ge(small_in, 32)
            nc.scalar.activation(wsm_hi[:], wsm[:], ACT.Copy).then_inc(pre_act, 1)
            for k in range(KT):
                act.wait_ge(tr_ready, k // 2 + 1)
                if k == 0:
                    act.wait_ge(pre_dve, 2)
                nc.scalar.activation(h_hi[:, k, :], ps[2 + k // 2][:, (k % 2) * SEQ:(k % 2 + 1) * SEQ], ACT.Copy,
                                     scale=cols_b[:, ROW_N1 + k:ROW_N1 + k + 1]).then_inc(h_hi_done, 1)

            def small_gates():
                act.wait_ge(cols_ready, 1)
                link(nc.scalar.activation(col["t0"][:], col["t0"][:], ACT.Exp))
                link(nc.scalar.activation(col["t0"][:], col["t0"][:], ACT.Ln, bias=ones[:, 0:1]))
                act.wait_ge(misc_in, 96)
                nc.scalar.activation(par[:, 0, :], par[:, 0, :], ACT.Exp)
                nc.scalar.activation(col["beta"][:], small[:, :, HEADS:2 * HEADS].rearrange("p t h -> p h t"), ACT.Tanh, scale=0.5)
                nc.scalar.activation(gates[:], small[:, :, 2 * HEADS:], ACT.Tanh, scale=0.5).then_inc(pre_act, 1)
                act.wait_ge(cols_ready, 2)
                nc.scalar.activation(col["eg"][:], col["gc"][:], ACT.Exp)
                nc.scalar.activation(col["kf"][:], col["gl"][:], ACT.Exp).then_inc(pre_act, 1)

            def evacuate(n):
                kind, i = CHUNKS[n]
                if n not in BANK_USE:
                    return
                u = BANK_USE[n]
                bank = stream_ps[u % 2][:].rearrange("p (a c) -> p a c", a=2)
                act.wait_ge(half_done, 2 * n + 2)
                if kind in ("gk", "gq", "gv"):
                    k = {"gk": 0, "gq": 4, "gv": 8}[kind] + i
                    if k >= 2:
                        act.wait_ge(conv_acc, k - 1)
                    else:
                        act.wait_ge(pre_dve, 1)
                    nc.scalar.activation(cin[k % 2][:, :, 3:3 + SEQ], bank, ACT.Copy).then_inc(copied, 1)
                elif kind == "gz":
                    if i == 0:
                        act.wait_ge(colsum, 12)
                    else:
                        act.wait_ge(zs_done, i)
                    nc.scalar.activation(gate_t[:], bank, ACT.Tanh, scale=0.5).then_inc(zt, 1)
                elif kind == "nq":
                    nc.scalar.activation(nqT[:, 2 * i:2 * i + 2, :], bank, ACT.Copy).then_inc(copied, 1)
                    act.wait_ge(copied, COPY_NO[n] + 1)
                    if i >= 1:
                        act.wait_ge(colsum, 8 + i)
                    nc.scalar.activation(nsq[:], nqT[:, 2 * i:2 * i + 2, :], ACT.Square).then_inc(nq_sq, 1)
                elif kind in ("ks", "kw"):
                    j = 0 if kind == "ks" else 1
                    nc.scalar.activation(key_tok[:, j, :, :].rearrange("p a d -> p (a d)"), stream_ps[u % 2][:], ACT.Copy).then_inc(copied, 1)
                    act.wait_ge(copied, COPY_NO[n] + 1)
                    for q in range(4):
                        nc.scalar.activation(sc[j][:].rearrange("p a c -> p (a c)")[:, q * DH:(q + 1) * DH], key_tok[:, j, q, :], ACT.Square,
                                             accum_out=ksum[:, 4 * j + q:4 * j + q + 1]).then_inc(key_in, 1)
                elif kind in ("vs", "vw"):
                    dst = vs if kind == "vs" else vw
                    nc.scalar.activation(dst[:].rearrange("p t g d -> p (t g d)"), stream_ps[u % 2][:], ACT.Copy).then_inc(copied, 1)
                elif kind in ("kc", "vc"):
                    j = 0 if kind == "kc" else 1
                    nc.scalar.activation(cmp_raw[:, j, :, :], bank, ACT.Copy).then_inc(copied, 1)
                elif kind in ("mga", "mgb"):
                    j = i + (4 if kind == "mgb" else 0)
                    if kind == "mga":
                        act.wait_ge(pa_done if i else zs_done, i if i else 4)
                    else:
                        act.wait_ge(pb_read if i else pa_done, i if i else 4)
                    nc.scalar.activation(gate_t[:], bank, ACT.Tanh, scale=0.5).then_inc(mg_done, 1)
                elif kind == "pb":
                    act.wait_ge(mix_done, i + 1)
                    nc.scalar.activation(mix_hi[:, 2 * i:2 * i + 2, :], mix[:, 2 * i:2 * i + 2, :], ACT.Copy, scale=0.5).then_inc(mix_hi_done, 1)
                elif kind == "gu":
                    if i >= 2:
                        act.wait_ge(gu_done, i - 1)
                    nc.scalar.activation(sg[i % 2][:], bank[:, 0, :], ACT.Silu).then_inc(sg_done, 1)
                    act.wait_ge(gu_done, i + 1)
                    if i >= 4:
                        act.wait_ge(half_done, 2 * AT["dn", (i - 4) // 2] + 1 + i % 2)
                    nc.scalar.activation(g_hi[i % 4][:], gu[i % 2][:], ACT.Copy).then_inc(g_hi_done, 1)

            def conv_step(k, part):
                if part == 0:
                    act.wait_ge(conv_acc, k + 1)
                    nc.scalar.activation(cth[k % 2][:], cacc[k % 2][:], ACT.Tanh, scale=0.5).then_inc(conv_th, 1)
                elif k < 8:
                    act.wait_ge(conv_done, k + 1)
                    if k >= 2:
                        act.wait_ge(colsum, k - 1)
                    src = (kT if k < 4 else qT)[:, 4 * (2 * (k % 4)) // 2:4 * (2 * (k % 4)) // 2 + 4, :]
                    nc.scalar.activation(csq[k % 2][:].rearrange("p a (t c) -> p (a t) c", t=TT), src, ACT.Square).then_inc(conv_sq, 1)

            def gdn(name):
                for b in range(NB):
                    u = stage_use(name, b)
                    bank, done = gdn_ps[u % GRING], g_out[u % GRING]
                    b4 = bank[:].rearrange("p (q c) -> p q c", q=4)
                    if name == "row":
                        act.wait_ge(done, u // GRING + 1)
                        nc.scalar.activation(problems(ET, b), problems(ET, b), ACT.Exp).then_inc(et_ready, 1)
                    elif name in ("knT", "at") or name[0] == "X":
                        dst = {"k": kT, "a": ATb, "X": AXb}[name[0]]
                        act.wait_ge(g_mm, u + 1)
                        if name == "X1":
                            act.wait_ge(lvl0, b + 1)
                        nc.scalar.activation(problems(dst, b), b4, ACT.Copy).then_inc(done, 1)
                    elif name == "w0":
                        act.wait_ge(g_mm, u + 1)
                        link(nc.scalar.activation(problems(AXb, b)[:, 0:4:2, :], b4[:, 0:2, :], ACT.Copy))
                        nc.scalar.activation(problems(Db, b)[:, 1:4:2, :], b4[:, 2:4, :], ACT.Copy, scale=-1.0).then_inc(done, 1)
                    elif name == "v1":
                        act.wait_ge(g_mm, u + 1)
                        link(nc.scalar.activation(problems(AXb, b)[:, 1:4:2, :], b4[:, 0:2, :], ACT.Copy))
                        for hh in range(2):
                            h = 2 * b + hh
                            ins = nc.scalar.activation(problems(Db, b)[:, 2 * hh + 1, :], b4[:, 2 + hh, :], ACT.Copy,
                                                       scale=col["eg"][:, h, 1:2])
                            if hh == 0:
                                link(ins)
                            else:
                                ins.then_inc(done, 1)
                    elif name == "o1":
                        act.wait_ge(o_ready, b + 1)
                        for q in range(4):
                            ins = nc.scalar.activation(problems(kn, b)[:, q, :], problems(kT, b)[:, q, :], ACT.Square,
                                                       accum_out=pcol("ss", b)[:, q:q + 1]).then_inc(ss_ready, 1)

            def misc(m):
                if m in (TURN_KS, TURN_KW):
                    act.wait_ge(m_pe, m + 1)
                    j = m - TURN_KS
                    dst = (ksT, kwT)[j][:].rearrange("p g (t c) -> p t g c", t=TT)
                    nc.scalar.activation(dst, log_ps[:].rearrange("p (t g c) -> p t g c", t=TT, g=GROUPS), ACT.Copy,
                                         scale=wk[:, 1 + j:2 + j]).then_inc(m_out, 1)
                elif m == TURN_KC:
                    act.wait_ge(m_pe, m + 1)
                    nc.scalar.activation(kcT[:, :, 0:NCMP], log_ps[:, 0:32].rearrange("p (g c) -> p g c", g=GROUPS)[:, :, 0:NCMP],
                                         ACT.Copy, scale=wk[:, 0:1]).then_inc(m_out, 1)
                elif m == W2_V:
                    act.wait_ge(m_pe, m + 1)
                    nc.scalar.activation(vc[:].rearrange("p g d -> p (g d)"), log_ps[0:NCMP, 0:GROUPS * DH], ACT.Copy).then_inc(m_out, 1)
                elif m == LOGITS_C:
                    act.wait_ge(pc_s, 1)
                    nc.scalar.activation(pc[:], pc[:], ACT.Exp).then_inc(pc_e, 1)
                elif m >= TURN_PC:
                    act.wait_ge(m_pe, m + 1)
                    q = 4 * (m - TURN_PC)
                    nc.scalar.activation(pcT[:, q:q + 4, :], log_ps[0:NCMP, :].rearrange("p (a c) -> p a c", a=4), ACT.Copy).then_inc(m_out, 1)

            def hidden(c):
                act.wait_ge(half_done, 2 * AT["cmpk" if c == 0 else "cmpv", 3] + 2)
                for a in range(2):
                    nc.scalar.activation(hid[:, c, a, :], ps[6 + a][:, 0:32], ACT.Tanh, scale=0.5).then_inc(hid_th, 1)

            def unit(i):
                if i < len(UNITS):
                    h, t = UNITS[i]
                    w = P * (t + 1)
                    act.wait_ge(s_done, i + 1)
                    for a in range(2):
                        nc.scalar.activation(sc[i % 2][:, a, 0:w], sc[i % 2][:, a, 0:w], ACT.Exp,
                                             bias=scol["nm"][:, 2 * (i % 2) + a:2 * (i % 2) + a + 1],
                                             accum_out=scol["se"][:, 2 * (i % 2) + a:2 * (i % 2) + a + 1]).then_inc(e_done, 1)
                if 1 <= i <= len(UNITS):
                    j = i - 1
                    h, t = UNITS[j]
                    act.wait_ge(t_mm, j + 1)
                    if j >= 2:
                        act.wait_ge(v_mm, j - 1)
                    nb = 2 * (t + 1)
                    nc.scalar.activation(pt[j % 2][:, 0:nb, :], pt_ps[:].rearrange("p (a c) -> p a c", a=4)[:, 0:nb, :], ACT.Copy).then_inc(t_out, 1)
                if i >= 2:
                    j = i - 2
                    h, t = UNITS[j]
                    act.wait_ge(v_mm, j + 1)
                    nc.scalar.activation(nqT[:, h, t * P:(t + 1) * P], pv_ps[:, 0:P], ACT.Copy).then_inc(v_out, 1)

            for n in range(len(CHUNKS) + 1):
                kind, i = CHUNKS[n] if n < len(CHUNKS) else (None, 0)
                if n == 0:
                    split_hi(1)
                    small_gates()
                else:
                    evacuate(n - 1)
                    if n + 1 < len(CHUNKS):
                        split_hi(n + 1)
                if 1 <= n <= 12:
                    conv_step(n - 1, 0)
                    conv_step(n - 1, 1)
                for half in range(2):
                    for name in slot_stages(n, half):
                        gdn(name)
                    if half == 0 and n - 1 in (AT["cmpk", 3], AT["cmpv", 3]):
                        hidden(0 if n - 1 == AT["cmpk", 3] else 1)
                    for m in slot_misc(n, half):
                        misc(m)
                    for i in slot_units(n, half):
                        unit(i)
                if n == AT["mga", 0]:
                    act.wait_ge(zs_done, 4 + NB)
                    for b in range(NB):
                        nc.scalar.activation(ya_hi[:, 2 * b:2 * b + 2, :], zsT[:, 2 * b:2 * b + 2, :], ACT.Copy).then_inc(ya_hi_done, 1)
                if n == AT["pa", 0]:
                    act.wait_ge(g_mm, NB * len(STAGES))
                    act.dma_start(x1[:], x[0].rearrange("(t p) d -> p t d", p=P)).then_inc(xres_in, 16)
                if n == AT["mgb", 0]:
                    act.wait_ge(v_out, len(UNITS))
                    for b in range(NB):
                        nc.scalar.activation(yb_hi[:, 2 * b:2 * b + 2, :], nqT[:, 2 * b:2 * b + 2, :], ACT.Copy).then_inc(yb_hi_done, 1)
                if n == AT["gu", 0]:
                    act.wait_ge(x1_done, 4)
                    for t in range(TT):
                        nc.scalar.activation(x1n[:, t, :], x1[:, t, :], ACT.Square, accum_out=scol["x"][:, t:t + 1]).then_inc(xss, 1)
                    for k in range(KT):
                        act.wait_ge(tr_ready, 4 + k // 2 + 1)
                        nc.scalar.activation(h_hi[:, k, :], ps[2 + k // 2][:, (k % 2) * SEQ:(k % 2 + 1) * SEQ], ACT.Copy,
                                             scale=cols_b[:, ROW_N2 + k:ROW_N2 + k + 1]).then_inc(h_hi_done, 1)

        @block.vector
        def _(dve):
            count = [0]

            def link(ins):
                count[0] += 1
                ins.then_inc(dve_step, 1)
                dve.wait_ge(dve_step, count[0])

            def split_lo(n):
                dve.wait_ge(raw_in[n % NRAW], 16 * loads_before(n))
                dve.wait_ge(hi_done, n + 1)
                nc.vector.tensor_tensor(w_lo[n % NSPL][:], raw[n % NRAW][:], w_hi[n % NSPL][:].bitcast(f32),
                                        ALU.subtract).then_inc(lo_done, 1)

            def rsqrt(y, xx, u, done=None):
                link(nc.vector.tensor_scalar(u.bitcast(i32), xx.bitcast(i32), 1, None, ALU.logical_shift_right))
                link(nc.vector.tensor_scalar(y.bitcast(i32), u.bitcast(i32), -1, 0x5F3759DF, ALU.mult, ALU.add))
                for k in range(3):
                    link(nc.vector.tensor_tensor(u, y, y, ALU.mult))
                    link(nc.vector.scalar_tensor_tensor(u, u, -0.5, xx, ALU.mult, ALU.mult))
                    last = nc.vector.scalar_tensor_tensor(y, u, 1.5, y, ALU.add, ALU.mult)
                    if done is None or k < 2:
                        link(last)
                    else:
                        last.then_inc(done, 1)

            def normalise(src, dst, norms_before):
                dve.wait_ge(xss, norms_before + TT)
                link(nc.vector.tensor_scalar(scol["x"][:, 2:4], scol["x"][:, 0:2], 1.0 / D_MODEL, EPS, ALU.mult, ALU.add))
                rsqrt(scol["x"][:, 4:6], scol["x"][:, 2:4], scol["x"][:, 6:8])
                for t in range(TT):
                    nc.vector.tensor_scalar(dst[:, t, :], src[:, t, :], scol["x"][:, 4 + t:5 + t], None, ALU.mult).then_inc(xn_done, 1)

            def h_low(before, row):
                for k in range(KT):
                    dve.wait_ge(h_hi_done, before + 2 * (k // 2) + 2)
                    nc.vector.scalar_tensor_tensor(h_lo[:, k, :], ps[2 + k // 2][:, (k % 2) * SEQ:(k % 2 + 1) * SEQ],
                                                   cols_b[:, row + k:row + k + 1], h_hi[:, k, :].bitcast(f32),
                                                   ALU.mult, ALU.subtract).then_inc(h_lo_done, 1)

            nc.vector.memset(cin[0][:, :, 0:3], 0.0)
            nc.vector.memset(cin[1][:, :, 0:3], 0.0).then_inc(pre_dve, 1)
            dve.wait_ge(pre_pe, 2)
            link(nc.vector.tensor_copy(cols_a[:], ps[7][:, 0:CONV * 24]))
            nc.vector.tensor_copy(cols_b[:], ps[7][:, P:P + NROWS]).then_inc(pre_dve, 1)
            dve.wait_ge(pre_dve, 2)
            link(nc.vector.tensor_scalar(wk[:], cols_b[:, ROW_KN:ROW_KN + 3], cols_b[:, ROW_QN:ROW_QN + 1], DH ** -0.5, ALU.mult, ALU.mult))
            link(nc.vector.tensor_scalar(zw[:], cols_b[:, ROW_GDN:ROW_GDN + 1], 0.5, None, ALU.mult))
            normalise(x_sb, xn_sb, 0)
            split_lo(0)
            dve.wait_ge(pre_act, 1)
            nc.vector.tensor_tensor(wsm_lo[:], wsm[:], wsm_hi[:].bitcast(f32), ALU.subtract).then_inc(pre_dve, 1)
            h_low(0, ROW_N1)
            dve.wait_ge(pre_pe, 3)
            nc.vector.tensor_copy(bias_v[:], ps[6][0:HEADS, 0:384]).then_inc(pre_dve, 1)

            def small_gates():
                dve.wait_ge(pre_pe, 4)
                link(nc.vector.tensor_copy(small[:].rearrange("p t c -> p (t c)"), ps[7][:, 256:256 + TT * NSMALL]))
                dve.wait_ge(misc_in, 96)
                a = small[:, :, 0:HEADS].rearrange("p t h -> p h t")
                link(nc.vector.tensor_tensor(col["t1"][:], a, par[:, 1, :].unsqueeze(2).to_broadcast([P, HEADS, TT]), ALU.add))
                link(nc.vector.tensor_scalar(col["t2"][:], col["t1"][:], -1.0, None, ALU.mult))
                nc.vector.tensor_tensor(col["t0"][:], col["t1"][:], col["t2"][:], ALU.min).then_inc(cols_ready, 1)
                link(nc.vector.tensor_scalar(col["t1"][:], col["t1"][:], 0.0, None, ALU.max))
                dve.wait_ge(pre_act, 2)
                link(nc.vector.tensor_tensor(col["t1"][:], col["t1"][:], col["t0"][:], ALU.add))
                link(nc.vector.scalar_tensor_tensor(col["g"][:], col["t1"][:], -1.0, par[:, 0, :].unsqueeze(2).to_broadcast([P, HEADS, TT]), ALU.mult, ALU.mult))
                link(nc.vector.tensor_scalar(col["beta"][:], col["beta"][:], 0.5, 0.5, ALU.mult, ALU.add))
                nc.vector.tensor_scalar(col["hbeta"][:], col["beta"][:], 0.5, None, ALU.mult)
                nc.vector.tensor_scalar(col["nbeta"][:], col["beta"][:], -1.0, None, ALU.mult)
                nc.vector.tensor_scalar(gates[:], gates[:], 0.5, 0.5, ALU.mult, ALU.add).then_inc(pre_dve, 1)
                dve.wait_ge(pre_pe, 5)
                link(nc.vector.tensor_copy(col["gc"][:].rearrange("p h t -> p (h t)"), ps[7][:, 384:400]))
                nc.vector.tensor_tensor(col["gl"][:].rearrange("p h t -> p (h t)"), ps[7][:, 400:416],
                                        col["gc"][:].rearrange("p h t -> p (h t)"), ALU.subtract).then_inc(cols_ready, 1)
                dve.wait_ge(pre_act, 3)
                link(nc.vector.tensor_tensor(col["kf"][:, :, 1], col["beta"][:, :, 1], col["eg"][:, :, 1], ALU.mult))

            def conv(k):
                dve.wait_ge(copied, k + 1)
                for a in range(2):
                    tile_no = {0: 8, 1: 0, 2: 16}[k // 4] + 2 * (k % 4) + a
                    w = lambda j: cols_a[:, j * 24 + tile_no:j * 24 + tile_no + 1]
                    acc, src = cacc[k % 2][:, a, :], cin[k % 2]
                    link(nc.vector.tensor_scalar(acc, src[:, a, 0:SEQ], w(0), None, ALU.mult))
                    for j in range(1, CONV):
                        ins = nc.vector.scalar_tensor_tensor(acc, src[:, a, j:j + SEQ], w(j), acc, ALU.mult, ALU.add)
                        if j == CONV - 1 and a == 1:
                            ins.then_inc(conv_acc, 1)
                        else:
                            link(ins)
                dve.wait_ge(conv_th, k + 1)
                dst = (kT, qT, vT)[k // 4][:, 4 * (k % 4):4 * (k % 4) + 4, :]
                v = lambda t: t[:].rearrange("p a (t c) -> p (a t) c", t=TT)
                nc.vector.scalar_tensor_tensor(dst, v(cth[k % 2]), 1.0, v(cacc[k % 2]), ALU.add, ALU.mult).then_inc(conv_done, 1)

            def inverse_norm(name, bank, scale, eps, after):
                f = lambda n: col[n][:].rearrange("p h t -> p (h t)")
                link(nc.vector.tensor_scalar(f("t1"), bank[:, 0:16], scale, eps, ALU.mult, ALU.add))
                rsqrt(f(name), f("t1"), f("t2"))
                return nc.vector.tensor_scalar(f(name), f(name), after, None, ALU.mult)

            def gdn(name):
                for b in range(NB):
                    u = stage_use(name, b)
                    bank, done = gdn_ps[u % GRING], g_out[u % GRING]
                    b4 = bank[:].rearrange("p (q c) -> p q c", q=4)
                    mine = name in ("row", "kt", "vt", "gram", "kq", "m1t", "s1", "o1", "ot") or name[0] in "YZ"
                    if mine:
                        dve.wait_ge(g_mm, u + 1)
                    if name == "row":
                        for q in range(4):
                            ins = nc.vector.scalar_tensor_tensor(problems(ET, b)[:, q, :], b4[:, q, :], pcol("gc", b)[:, q:q + 1],
                                                                 negmask[:], ALU.subtract, ALU.add)
                        ins.then_inc(done, 1)
                    elif name == "kt":
                        nc.vector.tensor_tensor(problems(kn, b), b4, wide_col("rk", b), ALU.mult).then_inc(done, 1)
                    elif name == "vt":
                        nc.vector.tensor_tensor(problems(vT, b), b4, wide_col("hbeta", b), ALU.mult).then_inc(done, 1)
                    elif name == "gram":
                        dve.wait_ge(et_ready, b + 1)
                        nc.vector.tensor_tensor(problems(AXb, b), b4, problems(ET, b), ALU.mult).then_inc(done, 1)
                    elif name == "kq":
                        nc.vector.tensor_tensor(problems(ET, b), b4, problems(ET, b), ALU.mult).then_inc(done, 1)
                    elif name == "m1t":
                        nc.vector.tensor_tensor(problems(AXb, b), b4, wide_col("nbeta", b), ALU.mult).then_inc(done, 1)
                    elif name == "at":
                        wait_use(dve, "at", b)
                        if b == 0:
                            dve.wait_ge(d_init, 2)
                            dve.wait_ge(levels_in, 16)
                        m = lambda l: levels[:, l, :].unsqueeze(1).to_broadcast([P, 4, P])
                        nc.vector.copy_predicated(problems(Db, b), m(0), problems(AXb, b))
                        nc.vector.copy_predicated(problems(DTb, b), m(LEVELS), problems(ATb, b)).then_inc(lvl0, 1)
                    elif name[0] in "YZ":
                        l = int(name[1:])
                        m = levels[:, l + (LEVELS if name[0] == "Z" else 0), :].unsqueeze(1).to_broadcast([P, 4, P])
                        nc.vector.copy_predicated(problems(Db if name[0] == "Y" else DTb, b), m, b4).then_inc(done, 1)
                    elif name == "s1":
                        link(nc.vector.tensor_copy(problems(Db, b)[:, 0:4:2, :], b4[:, 0:2, :]))
                        nc.vector.tensor_tensor(problems(kT, b)[:, 0:4:2, :], b4[:, 2:4, :],
                                                pcol("rq", b)[:, 0:4:2].unsqueeze(2).to_broadcast([P, 2, P]), ALU.mult).then_inc(done, 1)
                    elif name == "o1":
                        nc.vector.tensor_tensor(problems(kT, b)[:, 1:4:2, :], b4[:, 0:2, :], problems(Db, b)[:, 1:4:2, :],
                                                ALU.add).then_inc(done, 1)
                        wait_use(dve, "o1", b)
                        nc.vector.tensor_tensor(problems(kT, b)[:, 1:4:2, :], problems(kT, b)[:, 1:4:2, :],
                                                pcol("rq", b)[:, 1:4:2].unsqueeze(2).to_broadcast([P, 2, P]), ALU.mult).then_inc(o_ready, 1)
                        dve.wait_ge(ss_ready, 4 * b + 4)
                        link(nc.vector.tensor_scalar(pcol("t1", b), pcol("ss", b), 1.0 / DH, EPS, ALU.mult, ALU.add))
                        rsqrt(pcol("of", b), pcol("t1", b), pcol("t2", b), of_ready)
                    elif name == "ot":
                        dve.wait_ge(zs_done, 4)
                        z = zsT[:, 2 * b:2 * b + 2, :].rearrange("p h (t c) -> p (h t) c", t=TT)
                        nc.vector.scalar_tensor_tensor(z, b4, zw[:], z, ALU.mult, ALU.mult).then_inc(zs_done, 1)

            def keys(j):
                dve.wait_ge(key_in, 4 * j + 4)
                link(nc.vector.tensor_scalar(kr[:, 4 * j:4 * j + 4], ksum[:, 4 * j:4 * j + 4], 1.0 / DH, EPS, ALU.mult, ALU.add))
                rsqrt(scol["c"][:, 4 * j:4 * j + 4], kr[:, 4 * j:4 * j + 4], scol["d"][:, 0:4])
                nc.vector.tensor_tensor(key_tok[:, j, :, :], key_tok[:, j, :, :],
                                        scol["c"][:, 4 * j:4 * j + 4].unsqueeze(2).to_broadcast([P, 4, DH]), ALU.mult).then_inc(key_n, 1)

            def flatten(c):
                dve.wait_ge(copied, COPY_NO[AT["kc" if c == 0 else "vc", 0]] + 1)
                if c == 1:
                    dve.wait_ge(half_done, 2 * AT["cmpk", 3] + 2)
                link(nc.vector.memset(sc[0][:].rearrange("p a c -> p (a c)"), 0.0))
                for r in range(2):
                    s = sc[0][:].rearrange("p a c -> p (a c)").rearrange("p (j g n) -> p j g n", j=16, g=GROUPS)
                    for g in range(GROUPS):
                        src = cmp_raw[:, c, g, :].rearrange("p (n j) -> p j n", j=CMP_STRIDE)[:, :, r:r + NCMP]
                        e = cols_b[:, ROW_PE + c * CMP_BLOCK + r * 16:ROW_PE + c * CMP_BLOCK + (r + 1) * 16]
                        link(nc.vector.tensor_tensor(s[:, :, g, 0:NCMP], src, e.unsqueeze(2).to_broadcast([P, 16, NCMP]), ALU.add))
                    sf = sc[0][:].rearrange("p a c -> p (a c)").rearrange("p (j m) -> p j m", j=16)
                    link(nc.vector.tensor_copy(flat_hi[:, 16 * r:16 * r + 16, :], sf))
                    ins = nc.vector.tensor_tensor(flat_lo[:, 16 * r:16 * r + 16, :], sf, flat_hi[:, 16 * r:16 * r + 16, :].bitcast(f32), ALU.subtract)
                    if r == 1:
                        ins.then_inc(flat_done, 1)
                    else:
                        link(ins)

            def hidden(c):
                dve.wait_ge(hid_th, 2 * c + 2)
                for a in range(2):
                    link(nc.vector.scalar_tensor_tensor(hid[:, c, a, :], hid[:, c, a, :], 1.0, ps[6 + a][:, 0:32], ALU.add, ALU.mult))
                nc.vector.tensor_scalar(hid[:, c, :, :], hid[:, c, :, :], 0.5, None, ALU.mult).then_inc(hid_done, 1)

            def misc(m):
                if m == W2_K:
                    dve.wait_ge(m_pe, m + 1)
                    link(nc.vector.tensor_copy(kc[:].rearrange("p g d -> p (g d)"), log_ps[0:NCMP, 0:GROUPS * DH]))
                    for g in range(GROUPS):
                        link(nc.vector.tensor_tensor_reduce(sc[0][0:NCMP, 0, 0:DH], kc[:, g, :], kc[:, g, :], 1.0, 0.0, ALU.mult, ALU.add,
                                                            accum_out=scol["d"][0:NCMP, g:g + 1]))
                    link(nc.vector.tensor_scalar(scol["d"][0:NCMP, 2:4], scol["d"][0:NCMP, 0:2], 1.0 / DH, EPS, ALU.mult, ALU.add))
                    rsqrt(scol["d"][0:NCMP, 4:6], scol["d"][0:NCMP, 2:4], scol["d"][0:NCMP, 6:8])
                    nc.vector.tensor_tensor(kc[:], kc[:], scol["d"][0:NCMP, 4:6].unsqueeze(2).to_broadcast([NCMP, GROUPS, DH]), ALU.mult).then_inc(m_out, 1)
                elif m == LOGITS_C:
                    dve.wait_ge(m_pe, m + 1)
                    lg = log_ps[:, 0:HEADS * TT * 16].rearrange("p (h t n) -> p h t n", h=HEADS, t=TT)
                    link(nc.vector.memset(pc[:], NEG))
                    for t in range(TT):
                        k = NCMP if t else (P - CMP_BLOCK) // CMP_STRIDE + 1
                        first = P * (1 - t) + CMP_BLOCK - 1
                        link(nc.vector.tensor_tensor(pc[:, :, t, 0:k], lg[:, :, t, 0:k], col["rn"][:, :, t].unsqueeze(2).to_broadcast([P, HEADS, k]), ALU.mult))
                        link(nc.vector.tensor_tensor(pc[:, :, t, 0:k], pc[:, :, t, 0:k],
                                                     bias_g[:, :, first:first + CMP_STRIDE * (k - 1) + 1:CMP_STRIDE], ALU.add))
                    link(nc.vector.tensor_reduce(pcm[:].rearrange("p h t -> p (h t)"), pc[:].rearrange("p h t n -> p (h t) n"), AX.X, ALU.max))
                    nc.vector.tensor_tensor(pc[:].rearrange("p h t n -> p (h t) n"), pc[:].rearrange("p h t n -> p (h t) n"),
                                            pcm[:].rearrange("p h t -> p (h t)").unsqueeze(2).to_broadcast([P, 16, NCMP]), ALU.subtract).then_inc(pc_s, 1)
                    dve.wait_ge(pc_e, 1)
                    link(nc.vector.tensor_reduce(pcs[:].rearrange("p h t -> p (h t)"), pc[:].rearrange("p h t n -> p (h t) n"), AX.X, ALU.add))
                    link(nc.vector.reciprocal(pcs[:], pcs[:]))
                    link(nc.vector.tensor_scalar(pcs[:, :, 0], pcs[:, :, 0], rowvalid[:], None, ALU.mult))
                    g0 = gates[:].rearrange("p t (h b) -> p h t b", b=3)[:, :, :, 0]
                    link(nc.vector.tensor_tensor(pcs[:], pcs[:], g0, ALU.mult))
                    nc.vector.tensor_tensor(pc[:].rearrange("p h t n -> p (h t) n"), pc[:].rearrange("p h t n -> p (h t) n"),
                                            pcs[:].rearrange("p h t -> p (h t)").unsqueeze(2).to_broadcast([P, 16, NCMP]), ALU.mult).then_inc(m_out, 1)

            def unit(i):
                if i < len(UNITS):
                    h, t = UNITS[i]
                    w = P * (t + 1)
                    dve.wait_ge(l_mm, i + 1)
                    if i >= 2:
                        dve.wait_ge(t_mm, i - 1)
                    s = sc[i % 2][:, :, 0:w]
                    lg = log_ps[:].rearrange("p (a c) -> p a c", a=2)[:, :, 0:w]
                    bg = bias_g[:, h, SEQ - w:SEQ].unsqueeze(1).to_broadcast([P, 2, w])
                    link(nc.vector.scalar_tensor_tensor(s, lg, col["rn"][:, h, t:t + 1], bg, ALU.mult, ALU.add))
                    nc.vector.tensor_reduce(scol["nm"][:, 2 * (i % 2):2 * (i % 2) + 2], s, AX.X, ALU.max, negate=True).then_inc(s_done, 1)
                if 1 <= i <= len(UNITS):
                    j = i - 1
                    h, t = UNITS[j]
                    w = P * (t + 1)
                    dve.wait_ge(e_done, 2 * j + 2)
                    c2 = slice(2 * (j % 2), 2 * (j % 2) + 2)
                    link(nc.vector.reciprocal(scol["fac"][:, c2], scol["se"][:, c2]))
                    link(nc.vector.tensor_tensor(scol["fac"][:, c2], scol["fac"][:, c2], gates[:, t, 3 * h + 1:3 * h + 3], ALU.mult))
                    for a in range(2):
                        nc.vector.tensor_scalar(sc[j % 2][:, a, 0:w], sc[j % 2][:, a, 0:w], scol["fac"][:, 2 * (j % 2) + a:2 * (j % 2) + a + 1],
                                                None, ALU.mult).then_inc(p_done, 1)

            def evacuate(n):
                kind, i = CHUNKS[n]
                if n not in BANK_USE:
                    return
                u = BANK_USE[n]
                bank = stream_ps[u % 2][:].rearrange("p (a c) -> p a c", a=2)
                if kind == "gz":
                    dve.wait_ge(zt, i + 1)
                    nc.vector.scalar_tensor_tensor(zsT[:, 2 * i:2 * i + 2, :], gate_t[:], 1.0, bank, ALU.add, ALU.mult).then_inc(zs_done, 1)
                elif kind == "pa":
                    dve.wait_ge(mg_done, i + 1)
                    dve.wait_ge(half_done, 2 * n + 2)
                    nc.vector.scalar_tensor_tensor(mix[:, 2 * i:2 * i + 2, :], gate_t[:], 1.0, bank, ALU.add, ALU.mult).then_inc(pa_done, 1)
                elif kind == "pb":
                    dve.wait_ge(mg_done, 4 + i + 1)
                    dve.wait_ge(half_done, 2 * n + 2)
                    nc.vector.scalar_tensor_tensor(pmix[:], gate_t[:], 1.0, bank, ALU.add, ALU.mult).then_inc(pb_read, 1)
                    dve.wait_ge(pb_read, i + 1)
                    nc.vector.tensor_tensor(mix[:, 2 * i:2 * i + 2, :], mix[:, 2 * i:2 * i + 2, :], pmix[:], ALU.add).then_inc(mix_done, 1)
                    dve.wait_ge(mix_hi_done, i + 1)
                    nc.vector.scalar_tensor_tensor(mix_lo[:, 2 * i:2 * i + 2, :], mix[:, 2 * i:2 * i + 2, :], 0.5,
                                                   mix_hi[:, 2 * i:2 * i + 2, :].bitcast(f32), ALU.mult, ALU.subtract).then_inc(mix_lo_done, 1)
                elif kind == "wo":
                    dve.wait_ge(half_done, 2 * n + 2)
                    dve.wait_ge(xres_in, 16)
                    nc.vector.tensor_tensor(x1[:, :, i * CW:(i + 1) * CW], x1[:, :, i * CW:(i + 1) * CW], bank, ALU.add).then_inc(x1_done, 1)
                elif kind == "gu":
                    dve.wait_ge(sg_done, i + 1)
                    if i >= 2:
                        dve.wait_ge(g_hi_done, i - 1)
                    nc.vector.tensor_tensor(gu[i % 2][:], sg[i % 2][:], bank[:, 1, :], ALU.mult).then_inc(gu_done, 1)
                    dve.wait_ge(g_hi_done, i + 1)
                    nc.vector.tensor_tensor(g_lo[i % 4][:], gu[i % 2][:], g_hi[i % 4][:].bitcast(f32), ALU.subtract).then_inc(g_lo_done, 1)

            for n in range(len(CHUNKS) + 1):
                kind, _ = CHUNKS[n] if n < len(CHUNKS) else (None, 0)
                if n == 0:
                    split_lo(1)
                    small_gates()
                else:
                    if n > 12:
                        evacuate(n - 1)
                    if n + 1 < len(CHUNKS):
                        split_lo(n + 1)
                if 1 <= n <= 12:
                    conv(n - 1)
                if n == 2:
                    for i in range(4):
                        dve.wait_ge(bias_mm, i + 1)
                        nc.vector.tensor_copy(bias_g[:, 2 * i:2 * i + 2, :].rearrange("p h c -> p (h c)"), flip_ps[i][:]).then_inc(bias_done, 1)
                if n == 6:
                    dve.wait_ge(colsum, 4)
                    inverse_norm("rk", ps[5], 0.25, EPS, 0.5).then_inc(rk_ready, 1)
                    dve.wait_ge(rk_ready, 1)
                if n == 10:
                    dve.wait_ge(colsum, 8)
                    inverse_norm("rq", ps[6], 0.25, EPS, 0.5 * DH ** -0.5).then_inc(rq_ready, 1)
                    dve.wait_ge(rq_ready, 1)
                for half in range(2):
                    for name in slot_stages(n, half):
                        gdn(name)
                    if half == 0:
                        if n == AT["cmpv", 0]:
                            dve.wait_ge(colsum, 12)
                            inverse_norm("rn", ps[7], 1.0 / DH, EPS, 1.0).then_inc(rn_ready, 1)
                            dve.wait_ge(rn_ready, 1)
                        if n == AT["ks", 0] + 1:
                            keys(0)
                        if n == AT["kw", 0] + 1:
                            keys(1)
                        if n == AT["kc", 0] + 1:
                            flatten(0)
                        if n == AT["cmpk", 3] + 1:
                            hidden(0)
                            flatten(1)
                        if n == AT["cmpv", 3] + 1:
                            hidden(1)
                    for m in slot_misc(n, half):
                        misc(m)
                    for i in slot_units(n, half):
                        unit(i)
                if n == AT["mga", 0]:
                    for b in range(NB):
                        dve.wait_ge(ya_hi_done, b + 1)
                        nc.vector.tensor_tensor(ya_lo[:, 2 * b:2 * b + 2, :], zsT[:, 2 * b:2 * b + 2, :], ya_hi[:, 2 * b:2 * b + 2, :].bitcast(f32), ALU.subtract).then_inc(ya_lo_done, 1)
                if n == AT["mgb", 0]:
                    for b in range(NB):
                        dve.wait_ge(yb_hi_done, b + 1)
                        nc.vector.tensor_tensor(yb_lo[:, 2 * b:2 * b + 2, :], nqT[:, 2 * b:2 * b + 2, :], yb_hi[:, 2 * b:2 * b + 2, :].bitcast(f32), ALU.subtract).then_inc(yb_lo_done, 1)
                if n == AT["gu", 0]:
                    normalise(x1, x1n, TT)
                    h_low(KT, ROW_N2)
            for i in range(4):
                dve.wait_ge(half_done, 2 * len(CHUNKS))
                t, c = i // 2, i % 2
                nc.vector.tensor_tensor(out_sb[:, t, c * 512:(c + 1) * 512], x1[:, t, c * 512:(c + 1) * 512], ps[4 + i][:], ALU.add).then_inc(fin, 1)

        @block.tensor
        def _(pe):
            def three(pairs, bank, lhs, rhs, start, stop):
                (lh, ll), (rh, rl) = pairs
                pe.matmul(bank, lhs(lh), rhs(rh), start=start, stop=False)
                pe.matmul(bank, lhs(lh), rhs(rl), start=False, stop=False)
                return pe.matmul(bank, lhs(ll), rhs(rh), start=False, stop=stop)

            def transpose(o, i, n=P):
                return pe.transpose(o, i, ident[0:n, 0:n])

            def to_channels(src, before):
                pe.wait_ge(xn_done, before)
                for k in range(KT):
                    for t in range(TT):
                        o = (k % 2) * SEQ + t * P
                        last = transpose(ps[2 + k // 2][:, o:o + P], src[:, t, k * P:(k + 1) * P])
                    if k % 2:
                        last.then_inc(tr_ready, 1)

            pe.wait_ge(const_in, 48)
            pe.wait_ge(vec_in, 112)
            transpose(ps[7][:, 0:CONV * 24], rows_a[:], CONV * 24).then_inc(pre_pe, 1)
            transpose(ps[7][:, P:P + NROWS], rows_b[:], NROWS).then_inc(pre_pe, 1)
            to_channels(xn_sb, TT)
            pe.wait_ge(misc_in, 96)
            pe.matmul(ps[6][0:HEADS, 0:384], relb[:], onehot[:], start=True, stop=True).then_inc(pre_pe, 1)
            pe.wait_ge(h_hi_done, KT)
            pe.wait_ge(h_lo_done, KT)
            pe.wait_ge(pre_act, 1)
            pe.wait_ge(pre_dve, 3)
            for t in range(TT):
                for k in range(KT):
                    last = three(((h_hi, h_lo), (wsm_hi, wsm_lo)), ps[7][:, 256 + t * NSMALL:256 + (t + 1) * NSMALL],
                                 lambda a: a[:, k, t * P:(t + 1) * P], lambda a: a[:, k, :], k == 0, k == KT - 1)
            last.then_inc(pre_pe, 1)

            def decay_columns():
                pe.wait_ge(pre_dve, 5)
                pe.wait_ge(ones_set, 2)
                for t in range(TT):
                    pe.matmul(ps[7][:, 384 + t:400:2], upper[:], col["g"][:, :, t], start=True, stop=True)
                    last = pe.matmul(ps[7][:, 400 + t:416:2], ones_sq[:], col["g"][:, :, t], start=True, stop=True)
                last.then_inc(pre_pe, 1)

            def half_chunk(n, half):
                kind, i = CHUNKS[n]
                hi, lo = w_hi[n % NSPL], w_lo[n % NSPL]
                if half == 0:
                    pe.wait_ge(hi_done, n + 1)
                    pe.wait_ge(lo_done, n + 1)
                    wait_bank(pe, n)
                acts = (h_hi, h_lo)
                if kind == "pa":
                    acts = (ya_hi, ya_lo)
                    if n == AT["pa", 0] and half == 0:
                        pe.wait_ge(ya_hi_done, NB)
                        pe.wait_ge(ya_lo_done, NB)
                if kind == "pb":
                    acts = (yb_hi, yb_lo)
                    if n == AT["pb", 0] and half == 0:
                        pe.wait_ge(yb_hi_done, NB)
                        pe.wait_ge(yb_lo_done, NB)
                if kind == "wo":
                    acts = (mix_hi, mix_lo)
                    if n == AT["wo", 0] and half == 0:
                        pe.wait_ge(mix_hi_done, 4)
                        pe.wait_ge(mix_lo_done, 4)
                if n == AT["gu", 0] and half == 0:
                    to_channels(x1n, 2 * TT)
                    pe.wait_ge(h_hi_done, 2 * KT)
                    pe.wait_ge(h_lo_done, 2 * KT)
                if kind in ("cmpk", "cmpv"):
                    c = 0 if kind == "cmpk" else 1
                    if i == 0 and half == 0:
                        pe.wait_ge(flat_done, c + 1)
                        if c == 1:
                            pe.wait_ge(hid_done, 1)
                        else:
                            pe.wait_ge(rq_ready, 1)
                    if kind == "cmpv" and i == 0 and half == 1:
                        pe.wait_ge(rn_ready, 1)
                    for j in range(KT):
                        last = three(((hi, lo), (flat_hi, flat_lo)), ps[6 + half][:, 0:32],
                                     lambda a: a[:, j, half * P:(half + 1) * P] if a in (hi, lo) else None,
                                     lambda a: a[:, i * KT + j, :], i == 0 and j == 0, i == 3 and j == KT - 1)
                elif kind == "dn":
                    h2, l2 = (w[:].rearrange("p k c -> p (k c)").rearrange("p (k c) -> p k c", k=2) for w in (hi, lo))
                    tile_no = 2 * i + half
                    pe.wait_ge(g_hi_done, tile_no + 1)
                    pe.wait_ge(g_lo_done, tile_no + 1)
                    gh, gl = g_hi[tile_no % 4], g_lo[tile_no % 4]
                    for t in range(TT):
                        for c in range(2):
                            last = three(((gh, gl), (h2, l2)), ps[4 + 2 * t + c][:],
                                         lambda a: a[:, t * P:(t + 1) * P], lambda a: a[:, half, c * 512:(c + 1) * 512],
                                         tile_no == 0, tile_no == FFN // P - 1)
                else:
                    bank = stream_ps[BANK_USE[n] % 2][:, half * SEQ:(half + 1) * SEQ]
                    for k in range(KT):
                        if kind in TOKEN_MAJOR:
                            last = three((acts, (hi, lo)), bank, lambda a: a[:, k, half * P:(half + 1) * P], lambda a: a[:, k, :],
                                         k == 0, k == KT - 1)
                        else:
                            last = three(((hi, lo), acts), bank, lambda a: a[:, k, half * P:(half + 1) * P], lambda a: a[:, k, :],
                                         k == 0, k == KT - 1)
                return last

            def column_sums(sq, bank, first, is_ready, value):
                pe.wait_ge(is_ready, value)
                for a in range(2):
                    for t in range(TT):
                        last = pe.matmul(bank[:, first + 2 * a + t:first + 2 * a + t + 1], sq[:, a, t * P:(t + 1) * P], ones[:, 0:1],
                                         start=True, stop=True)
                last.then_inc(colsum, 1)

            def gdn(name):
                for b in range(NB):
                    u = stage_use(name, b)
                    if name == "ot" and b == GRING:
                        pe.wait_ge(zs_done, 4 + 1)
                    elif u >= GRING:
                        pe.wait_ge(g_out[u % GRING], u // GRING)
                    b4 = gdn_ps[u % GRING][:].rearrange("p (q c) -> p q c", q=4)
                    p4 = lambda t: problems(t, b)
                    mm = lambda q, lhsT, rhs, start=True, stop=True: pe.matmul(b4[:, q, :], lhsT, rhs, start=start, stop=stop)
                    if name == "row":
                        pe.wait_ge(pre_dve, 5)
                        if b == 0:
                            pe.wait_ge(rk_ready, 1)
                        for q in range(4):
                            last = mm(q, pcol("g", b)[:, q:q + 1].to_broadcast([P, P]), upper[:])
                    elif name in ("kt", "vt"):
                        pe.wait_ge(conv_done, b + 1 + (8 if name == "vt" else 0))
                        for q in range(4):
                            last = transpose(b4[:, q, :], p4(kT if name == "kt" else vT)[:, q, :])
                    elif name in ("knT", "m1t", "at", "ot"):
                        src, before = {"knT": (kn, "kt"), "m1t": (AXb, "gram"), "at": (AXb, "m1t"), "ot": (kT, None)}[name]
                        if before:
                            wait_use(pe, before, b)
                        else:
                            pe.wait_ge(on_ready, b + 1)
                        for q in range(4):
                            last = transpose(b4[:, q, :], p4(src)[:, q, :])
                    elif name in ("gram", "kq"):
                        wait_use(pe, "knT", b)
                        for q in range(4):
                            last = mm(q, p4(kT)[:, q, :], p4(kT if name == "gram" else qT)[:, q, :])
                    elif name[0] == "X":
                        l = int(name[1:])
                        if l == 1:
                            pe.wait_ge(lvl0, b + 1)
                        else:
                            wait_use(pe, f"Y{l - 1}", b)
                        for q in range(4):
                            last = mm(q, p4(ATb)[:, q, :], p4(Db)[:, q, :])
                    elif name[0] in "YZ":
                        l = int(name[1:])
                        wait_use(pe, f"X{l}", b)
                        if l > 1:
                            wait_use(pe, f"Z{l - 1}", b)
                        for q in range(4):
                            if name[0] == "Y":
                                last = mm(q, p4(DTb)[:, q, :], p4(AXb)[:, q, :])
                            else:
                                last = mm(q, p4(AXb)[:, q, :], p4(DTb)[:, q, :])
                    elif name == "w0":
                        wait_use(pe, f"Z{LEVELS - 1}", b)
                        wait_use(pe, "vt", b)
                        pe.wait_ge(kf_ready, b + 1)
                        for hh in range(2):
                            mm(hh, p4(DTb)[:, 2 * hh, :], p4(vT)[:, 2 * hh, :])
                        for hh in range(2):
                            last = mm(2 + hh, p4(kn)[:, 2 * hh + 1, :], p4(DTb)[:, 2 * hh + 1, :])
                    elif name == "s1":
                        wait_use(pe, "w0", b)
                        wait_use(pe, "kq", b)
                        for hh in range(2):
                            mm(hh, p4(kn)[:, 2 * hh, :], p4(AXb)[:, 2 * hh, :])
                        for hh in range(2):
                            last = mm(2 + hh, p4(ET)[:, 2 * hh, :], p4(AXb)[:, 2 * hh, :])
                    elif name == "v1":
                        wait_use(pe, "s1", b)
                        for hh in range(2):
                            mm(hh, p4(DTb)[:, 2 * hh + 1, :], p4(vT)[:, 2 * hh + 1, :], True, False)
                            mm(hh, p4(Db)[:, 2 * hh + 1, :], p4(Db)[:, 2 * hh, :], False, True)
                        for hh in range(2):
                            last = mm(2 + hh, p4(qT)[:, 2 * hh + 1, :], p4(Db)[:, 2 * hh, :])
                    elif name == "o1":
                        wait_use(pe, "v1", b)
                        for hh in range(2):
                            last = mm(hh, p4(ET)[:, 2 * hh + 1, :], p4(AXb)[:, 2 * hh + 1, :])
                    last.then_inc(g_mm, 1)

            def misc(m):
                if m >= 1:
                    pe.wait_ge(m_out, m)
                if m in (TURN_KS, TURN_KW):
                    j = m - TURN_KS
                    pe.wait_ge(key_n, j + 1)
                    for q in range(4):
                        last = transpose(log_ps[:, q * P:(q + 1) * P], key_tok[:, j, q, :])
                elif m in (W2_K, W2_V):
                    c = 0 if m == W2_K else 1
                    pe.wait_ge(hid_done, c + 1)
                    if c == 0:
                        pe.wait_ge(rk_ready, 1)
                    for g in range(GROUPS):
                        for a in range(2):
                            last = pe.matmul(log_ps[0:NCMP, g * DH:(g + 1) * DH], hid[:, c, a, g * 16:g * 16 + NCMP], cmp2[:, c, a, :],
                                             start=(a == 0), stop=(a == 1))
                elif m == TURN_KC:
                    for g in range(GROUPS):
                        last = transpose(log_ps[:, g * 16:g * 16 + NCMP], kc[:, g, :], NCMP)
                elif m == LOGITS_C:
                    pe.wait_ge(copied, COPY_NO[AT["nq", 3]] + 1)
                    for h in range(HEADS):
                        for t in range(TT):
                            o = (h * TT + t) * 16
                            last = pe.matmul(log_ps[:, o:o + NCMP], nqT[:, h, t * P:(t + 1) * P], kcT[:, h // 4, 0:NCMP], start=True, stop=True)
                else:
                    for q in range(4):
                        h, t = UNITS[4 * (m - TURN_PC) + q]
                        last = transpose(log_ps[0:NCMP, q * P:(q + 1) * P], pc[:, h, t, :])
                last.then_inc(m_pe, 1)

            def unit(i):
                if i < len(UNITS):
                    h, t = UNITS[i]
                    w = P * (t + 1)
                    if i >= 1:
                        pe.wait_ge(s_done, i)
                    else:
                        pe.wait_ge(m_out, 10)
                    for a, keys in enumerate((ksT, kwT)):
                        last = pe.matmul(log_ps[:, a * SEQ:a * SEQ + w], nqT[:, h, t * P:(t + 1) * P], keys[:, h // 4, 0:w], start=True, stop=True)
                    last.then_inc(l_mm, 1)
                if 1 <= i <= len(UNITS):
                    j = i - 1
                    h, t = UNITS[j]
                    pe.wait_ge(p_done, 2 * j + 2)
                    if j >= 1:
                        pe.wait_ge(t_out, j)
                    for a in range(2):
                        for k in range(t + 1):
                            o = (a * (t + 1) + k) * P
                            last = transpose(pt_ps[:, o:o + P], sc[j % 2][:, a, k * P:(k + 1) * P])
                    last.then_inc(t_mm, 1)
                if i >= 2:
                    j = i - 2
                    h, t = UNITS[j]
                    g = h // 4
                    pe.wait_ge(t_out, j + 1)
                    if j >= 1:
                        pe.wait_ge(v_out, j)
                    o = pv_ps[:, 0:P]
                    kk = NCMP if t else (P - CMP_BLOCK) // CMP_STRIDE + 1
                    pe.matmul(o, vc[0:kk, g, :], pcT[0:kk, j, :], start=True, stop=False)
                    for a, values in enumerate((vs, vw)):
                        for k in range(t + 1):
                            last = pe.matmul(o, values[:, k, g, :], pt[j % 2][:, a * (t + 1) + k, :], start=False, stop=(a == 1 and k == t))
                    last.then_inc(v_mm, 1)

            for n in range(len(CHUNKS)):
                kind, _ = CHUNKS[n]
                for half in range(2):
                    last = half_chunk(n, half)
                    last.then_inc(half_done, 1)
                    if n == 0 and half == 1:
                        decay_columns()
                    if n == 1 and half == 1:
                        pe.wait_ge(bias_in, 32)
                        for i in range(4):
                            pe.matmul(flip_ps[i][:], flip[:], bias_up[:, 2 * i:2 * i + 2, :].rearrange("p h c -> p (h c)"),
                                      start=True, stop=True).then_inc(bias_mm, 1)
                    if 2 <= n <= 9 and half == 0:
                        k = n - 2
                        if k == 4:
                            pe.wait_ge(bias_done, 4)
                        column_sums(csq[k % 2], ps[5] if k < 4 else ps[6], 4 * (k % 4), conv_sq, k + 1)
                    if AT["nq", 0] + 1 <= n <= AT["nq", 3] + 1 and half == 1:
                        k = n - AT["nq", 0] - 1
                        column_sums(nsq, ps[7], 4 * k, nq_sq, k + 1)
                    for name in slot_stages(n, half):
                        gdn(name)
                    for m in slot_misc(n, half):
                        misc(m)
                    for i in slot_units(n, half):
                        unit(i)


def shape_constants():
    i = np.arange(P)
    ident = np.eye(P, dtype=np.float32)
    upper = (i[:, None] <= i[None, :]).astype(np.float32)
    negmask = np.where(i[:, None] <= i[None, :], 0.0, NEG).astype(np.float32)
    levels = np.zeros((P, 2 * LEVELS, P), np.float32)
    for l in range(LEVELS):
        s = 1 << l
        m = (i[:, None] // (2 * s) == i[None, :] // (2 * s)) & (i[:, None] // s % 2 == 1) & (i[None, :] // s % 2 == 0)
        levels[:, l, :] = m
        levels[:, LEVELS + l, :] = m.T
    dist = SEQ - 1 - np.arange(384)
    d = np.maximum(dist, 0)
    exact = REL_BUCKETS // 2
    large = exact + (np.log(np.maximum(d, 1).astype(np.float32) / np.float32(exact)) / np.float32(math.log(REL_MAX_DIST / exact))
                     * np.float32(REL_BUCKETS - exact)).astype(np.int32)
    bucket = np.where(d < exact, d, np.minimum(large, REL_BUCKETS - 1))
    onehot = np.zeros((REL_BUCKETS + 1, 384), np.float32)
    onehot[bucket, np.arange(384)] = 1.0
    onehot[REL_BUCKETS, dist < 0] = NEG
    rowvalid = (i >= CMP_BLOCK - 1).astype(np.float32)[:, None]
    return {"c_ident": ident, "c_upper": upper, "c_negmask": negmask, "c_levels": levels, "c_onehot": onehot, "c_rowvalid": rowvalid,
            "c_flip": np.ascontiguousarray(ident[::-1])}


INS = ["x", "norm1_w", "w_in", "conv_w", "a_log", "dt_bias", "gdn_norm_w", "cmp_pe", "cmp_w1", "cmp_w2", "q_norm_w", "k_norm_w",
       "rel_bias", "w_proj_a", "w_proj_b", "w_out", "norm2_w", "w_gate", "w_up", "w_down"]


def kernel(**inputs):
    import concourse.bacc as bacc
    from concourse.bass_utils import run_bass_kernel_spmd

    nc = bacc.Bacc("TRN2", target_bir_lowering=False, num_devices=1)
    arrays = {n: np.ascontiguousarray(inputs[n]) for n in INS}
    arrays.update(shape_constants())
    args = [nc.dram_tensor("in_" + n, a.shape, mybir.dt.from_np(a.dtype), kind="ExternalInput").ap() for n, a in arrays.items()]
    scratch = nc.dram_tensor("bias_rows", [HEADS, 384], mybir.dt.float32, kind="Internal").ap()
    out = nc.dram_tensor("out_0", [1, SEQ, D_MODEL], mybir.dt.float32, kind="ExternalOutput").ap()
    hybrid_block(nc, *args, scratch, out)
    r = run_bass_kernel_spmd(nc, [{"in_" + n: a for n, a in arrays.items()}], core_ids=[0])
    return r.results[0]["out_0"]
```

```python
import math
from contextlib import ExitStack

import concourse.bass as bass
import numpy as np
from concourse import mybir

D_MODEL, SEQ = 1024, 256
HEADS, DH = 8, 128
GROUPS = 2
CMP_BLOCK, CMP_STRIDE, CMP_HIDDEN = 32, 16, 256
NCMP = SEQ // CMP_STRIDE - CMP_BLOCK // CMP_STRIDE + 1
CONV = 4
REL_BUCKETS, REL_MAX_DIST = 32, 1024
FFN = ((8 * D_MODEL + 3 * 256 - 1) // (3 * 256)) * 256
EPS = 1e-6
P = 128
TT = SEQ // P
KT = D_MODEL // P
CW = 256
LEVELS = int(math.log2(P))
NEG = -1e30

GQ, GK, GV, GZ = (i * D_MODEL for i in range(4))
GA = 4 * D_MODEL
NQ = GA + 2 * HEADS
NKV = NQ + D_MODEL
KV_W = GROUPS * DH
NGATE = NKV + 6 * KV_W
MGATE = NGATE + 3 * HEADS
NSMALL = 2 * HEADS + 3 * HEADS

ROW_N1, ROW_N2, ROW_GDN, ROW_QN, ROW_KN, ROW_PE = 0, KT, 2 * KT, 2 * KT + 1, 2 * KT + 2, 2 * KT + 5
NROWS = ROW_PE + 2 * CMP_BLOCK


def weight_chunks():
    out = [("gk", i) for i in range(4)] + [("gq", i) for i in range(4)] + [("gv", i) for i in range(4)]
    out += [("kc", 0), ("vc", 0)] + [("cmpk", i) for i in range(4)] + [("nq", i) for i in range(4)]
    out += [("ks", 0)] + [("cmpv", i) for i in range(4)] + [("vs", 0), ("kw", 0), ("vw", 0)] + [("gz", i) for i in range(4)]
    out += [("mga", 0), ("mga", 1), ("pa", 0), ("mga", 2), ("pa", 1), ("mga", 3), ("pa", 2), ("pa", 3)]
    for i in range(4):
        out += [("mgb", i), ("pb", i)]
    out += [("wo", i) for i in range(4)]
    nf = FFN // P
    for j in range(nf // 2):
        out += [("gu", 2 * j), ("gu", 2 * j + 1)]
        if j >= 1:
            out += [("dn", j - 1)]
    out += [("dn", nf // 2 - 1)]
    return out


CHUNKS = weight_chunks()
AT = {k: n for n, k in enumerate(CHUNKS)}
TOKEN_MAJOR = ("ks", "vs", "kw", "vw", "wo")
NO_BANK = ("cmpk", "cmpv", "dn")
COPIED = ("gk", "gq", "gv", "nq", "ks", "vs", "kw", "vw", "kc", "vc")
BANK_USE, COPY_NO = {}, {}
for _n, (_k, _i) in enumerate(CHUNKS):
    if _k not in NO_BANK:
        BANK_USE[_n] = len(BANK_USE)
    if _k in COPIED:
        COPY_NO[_n] = len(COPY_NO)
BANK_USER = {u: n for n, u in BANK_USE.items()}
LAST_OF_KIND = (("pb", 3), ("wo", 3))

STAGES = ["row", "kt", "vt", "knT", "gram", "kq", "m1t", "at"]
for _l in range(1, LEVELS):
    STAGES += [f"X{_l}"] + ([f"Y{_l}"] if _l < LEVELS - 1 else []) + [f"Z{_l}"]
STAGES += ["w0", "s1", "v1", "o1", "ot"]
NB = 4
GRING = 3


def stage_use(name, b):
    return NB * STAGES.index(name) + b


FIRST_STAGE_SLOT = AT["gv", 3] + 1
UNITS = [(h, t) for h in range(HEADS) for t in range(TT)]
FIRST_UNIT_SLOT = AT["gz", 1]


def slot_stages(n, half):
    if (n, half) == (AT["mga", 0], 1):
        return ["ot"]
    i = 2 * (n - FIRST_STAGE_SLOT) + half
    return [STAGES[i]] if 0 <= i < len(STAGES) - 1 else []


W2_K, TURN_KC, LOGITS_C, TURN_PC, W2_V, TURN_KS, TURN_KW = 0, 1, 2, 3, 7, 8, 9
MISC_SLOTS = {W2_K: (AT["nq", 1], 0), TURN_KC: (AT["nq", 2], 0), LOGITS_C: (AT["cmpv", 1], 1),
              TURN_PC: (AT["vs", 0], 1), TURN_PC + 1: (AT["kw", 0], 0), TURN_PC + 2: (AT["kw", 0], 1), TURN_PC + 3: (AT["vw", 0], 0),
              W2_V: (AT["vw", 0], 1),
              TURN_KS: (AT["gz", 0], 0), TURN_KW: (AT["gz", 0], 1)}


def slot_misc(n, half):
    return [m for m, where in MISC_SLOTS.items() if where == (n, half)]


def slot_units(n, half):
    i = 2 * (n - FIRST_UNIT_SLOT) + half
    return [i] if 0 <= i < len(UNITS) + 3 else []


def hybrid_block(nc, x, norm1_w, w_in, conv_w, a_log, dt_bias, gdn_norm_w, cmp_pe, cmp_w1, cmp_w2,
                 q_norm_w, k_norm_w, rel_bias, w_proj_a, w_proj_b, w_out, norm2_w, w_gate, w_up, w_down,
                 c_ident, c_upper, c_negmask, c_levels, c_onehot, c_rowvalid, c_flip, bias_rows, out):
    f32, f32r, i32, u8 = mybir.dt.float32, mybir.dt.float32r, mybir.dt.int32, mybir.dt.uint8
    ALU, ACT, AX = mybir.AluOpType, mybir.ActivationFunctionType, mybir.AxisListType
    ctx = ExitStack()
    with ctx:
        KB = 1024
        base = 16512
        cursor = [base]

        def at(name, addr, shape, dt=f32):
            return nc.alloc_sbuf_tensor_at(name, shape, dt, offset=addr)

        def take(nbytes):
            a = cursor[0]
            cursor[0] += (nbytes + 31) // 32 * 32
            return a

        def own(name, shape, dt=f32):
            n = int(np.prod(shape[1:])) * (1 if dt == u8 else 4)
            return at(name, take(n), shape, dt)

        NRAW, NSPL = 3, 2
        raw = [own(f"raw{i}", [P, KT, CW]) for i in range(NRAW)]
        w_hi = [own(f"w_hi{i}", [P, KT, CW], f32r) for i in range(NSPL)]
        w_lo = [own(f"w_lo{i}", [P, KT, CW], f32r) for i in range(NSPL)]
        h_hi, h_lo = own("h_hi", [P, KT, SEQ], f32r), own("h_lo", [P, KT, SEQ], f32r)
        yb_at = take(16 * KB)
        yb_hi, yb_lo = at("yb_hi", yb_at, [P, KT, SEQ], f32r), at("yb_lo", yb_at + 8 * KB, [P, KT, SEQ], f32r)
        cmp_raw = at("cmp_raw", yb_at, [P, 2, GROUPS, SEQ])
        flat_hi = at("flat_hi", yb_at + 4 * KB, [P, CMP_BLOCK, 32], f32r)
        flat_lo = at("flat_lo", yb_at + 8 * KB, [P, CMP_BLOCK, 32], f32r)
        key_tok = at("key_tok", yb_at + 12 * KB, [P, 2, 4, DH])
        pcT = at("pcT", yb_at, [NCMP, 16, P])
        arena = take(72 * KB)

        def ar(i, name, shape=(P, 16, P), dt=f32, off=0):
            return at(name, arena + i * 8 * KB + off, list(shape), dt)

        kT, qT, vT, kn, ET, AXb, ATb, Db, DTb = (ar(i, n) for i, n in enumerate(
            ["kT", "qT", "vT", "kn", "ET", "AXb", "ATb", "Db", "DTb"]))
        x_sb = ar(0, "x_sb", (P, TT, D_MODEL))
        xn_sb = ar(1, "xn_sb", (P, TT, D_MODEL))
        cin = [ar(5, f"cin{i}", (P, 2, SEQ + 8), off=i * 2112) for i in range(2)]
        cacc = [ar(6, f"cacc{i}", (P, 2, SEQ), off=i * 2 * KB) for i in range(2)]
        cth = [ar(6, f"cth{i}", (P, 2, SEQ), off=(2 + i) * 2 * KB) for i in range(2)]
        csq = [ar(7, f"csq{i}", (P, 2, SEQ), off=i * 2 * KB) for i in range(2)]
        ya_hi, ya_lo = ar(5, "ya_hi", (P, KT, SEQ), f32r), ar(6, "ya_lo", (P, KT, SEQ), f32r)
        mix = ar(7, "mix", (P, KT, SEQ))
        mix_hi, mix_lo = ar(3, "mix_hi", (P, KT, SEQ), f32r), ar(4, "mix_lo", (P, KT, SEQ), f32r)
        x1 = ar(0, "x1", (P, TT, D_MODEL))
        x1n = ar(1, "x1n", (P, TT, D_MODEL))
        sg = [ar(2, f"sg{i}", (P, SEQ), off=i * KB) for i in range(2)]
        gu = [ar(2, f"gu{i}", (P, SEQ), off=(2 + i) * KB) for i in range(2)]
        g_hi = [ar(8, f"g_hi{i}", (P, SEQ), f32r, off=i * KB) for i in range(4)]
        g_lo = [ar(8, f"g_lo{i}", (P, SEQ), f32r, off=(4 + i) * KB) for i in range(4)]
        out_sb = ar(1, "out_sb", (P, TT, D_MODEL))
        pmix = ar(8, "pmix", (P, 2, SEQ))

        z_at = cursor[0]
        zsT = own("zsT", [P, HEADS, SEQ])
        cmp2 = at("cmp2", z_at, [P, 2, 2, DH])
        kc = at("kc", z_at + 2 * KB, [NCMP, GROUPS, DH])
        pc = at("pc", z_at + 3 * KB, [P, HEADS, TT, NCMP])
        pcm = at("pcm", z_at + 4 * KB, [P, HEADS, TT])
        pcs = at("pcs", z_at + 4 * KB + 64, [P, HEADS, TT])
        nqT = own("nqT", [P, HEADS, SEQ])
        bias_up = at("bias_up", cursor[0] - 8 * KB, [P, HEADS, SEQ])
        bias_g = own("bias_g", [P, HEADS, SEQ])
        ksT, kwT = own("ksT", [P, GROUPS, SEQ]), own("kwT", [P, GROUPS, SEQ])
        vs, vw = own("vs", [P, TT, GROUPS, DH]), own("vw", [P, TT, GROUPS, DH])
        sc_at = take(4 * KB)
        sc = [at(f"sc{i}", sc_at + i * 2 * KB, [P, 2, SEQ]) for i in range(2)]
        pt_at = take(4 * KB)
        pt = [at(f"pt{i}", pt_at + i * 2 * KB, [P, 4, P]) for i in range(2)]
        sc.append(ar(1, "sc2", (P, 2, SEQ)))
        hid = at("hid", pt_at, [P, 2, 2, 32])
        hid_tok = at("hid_tok", pt_at + KB, [32, CW])
        rows_a = at("rows_a", sc_at, [CONV * 24, P])
        rows_b = at("rows_b", sc_at + 512, [NROWS, P])
        wsm = at("wsm", sc_at + KB, [P, KT, NSMALL])
        wsm_hi = at("wsm_hi", pt_at, [P, KT, NSMALL], f32r)
        wsm_lo = at("wsm_lo", pt_at + 1280, [P, KT, NSMALL], f32r)
        gate_t = own("gate_t", [P, 2, SEQ])
        gates_t = [gate_t, ar(2, "gate_u", (P, 2, SEQ), off=4 * KB)]
        nsq = at("nsq", cursor[0] - 2 * KB, [P, 2, SEQ])
        ident, upper, negmask = own("ident", [P, P]), own("upper", [P, P]), own("negmask", [P, P])
        vc = at("vc", cursor[0] - KB, [NCMP, GROUPS, DH])
        ones = own("ones", [P, 4])
        small_ch = ar(3, "small_ch", (NSMALL, SEQ))
        ones_sq = ar(8, "ones_sq", (P, P))
        cols_a = ar(8, "cols_a", (P, CONV * 24), off=512)
        flip = ar(8, "flip", (P, P), off=KB)
        levels = own("levels", [P, 2 * LEVELS, P], u8)
        onehot = at("onehot", sc_at + 2560, [REL_BUCKETS + 1, 384])
        relb = own("relb", [REL_BUCKETS + 1, HEADS])
        bias_v = at("bias_v", pt_at + 2560, [HEADS, 384])
        cols_b = own("cols_b", [P, NROWS])
        small = own("small", [P, TT, NSMALL])
        rowvalid = own("rowvalid", [P, 1])
        par = own("par", [P, 2, HEADS])
        col = {n: own("c_" + n, [P, HEADS, TT]) for n in (
            "g", "gc", "gl", "eg", "beta", "hbeta", "nbeta", "kf", "rk", "rq", "rn", "ss", "of", "t0", "t1", "t2")}
        gates = own("gates", [P, TT, 3 * HEADS])
        ksum = own("ksum", [P, 8])
        kr = own("kr", [P, 8])
        wk = own("wk", [P, 3])
        zw = own("zw", [P, 1])
        scol = {n: own("s_" + n, [P, 8]) for n in ("c", "d", "x", "nm", "se", "fac")}
        xs = own("xs", [P, TT, 4])
        kcT = own("kcT", [P, GROUPS, 16])

        ps = [ctx.enter_context(nc.psum_tensor(f"ps{i}", [P, 512], f32)) for i in range(8)]
        stream_ps = ps[0:2]
        gdn_ps = ps[2:5]
        log_ps, pt_ps, pv_ps = ps[5], ps[6], ps[7]

        def sem(name):
            return ctx.enter_context(nc.semaphore(name))

        raw_in = [sem(f"raw_in{i}") for i in range(NRAW)]
        hi_done, lo_done = sem("hi_done"), sem("lo_done")
        half_done = sem("half_done")
        copied = sem("copied")
        x_in, vec_in, ident_in, const_in, levels_in, small_in, misc_in = sem("x_in"), sem("vec_in"), sem("ident_in"), sem("const_in"), sem("levels_in"), sem("small_in"), sem("misc_in")
        bias_out, bias_in, bias_mm, bias_done = sem("bias_out"), sem("bias_in"), sem("bias_mm"), sem("bias_done")
        flip_ps = [ps[2], ps[3], ps[4], ps[6]]
        xres_in, out_done = sem("xres_in"), sem("out_done")
        ones_set, relb_set, d_init = sem("ones_set"), sem("relb_set"), sem("d_init")
        dve_step, act_step = sem("dve_step"), sem("act_step")
        pre_pe, pre_dve, pre_act = sem("pre_pe"), sem("pre_dve"), sem("pre_act")
        xss, xn_done = sem("xss"), sem("xn_done")
        tr_ready, h_hi_done, h_lo_done = sem("tr_ready"), sem("h_hi_done"), sem("h_lo_done")
        conv_acc, conv_th, conv_done, conv_sq, colsum = (sem(n) for n in (
            "conv_acc", "conv_th", "conv_done", "conv_sq", "colsum"))
        cols_ready, rk_ready, rq_ready, rn_ready = sem("cols_ready"), sem("rk_ready"), sem("rq_ready"), sem("rn_ready")
        g_mm = sem("g_mm")
        g_out = [sem(f"g_out{i}") for i in range(GRING)]
        et_ready, lvl0, kf_ready, ss_ready, on_ready = (sem(n) for n in (
            "et_ready", "lvl0", "kf_ready", "ss_ready", "on_ready"))
        small_raw, small_mm = sem("small_raw"), sem("small_mm")
        o_ready, of_ready, zt, zs_done = sem("o_ready"), sem("of_ready"), sem("zt"), sem("zs_done")
        nq_sq = sem("nq_sq")
        key_in, key_n = sem("key_in"), sem("key_n")
        flat_done = sem("flat_done")
        m_pe, m_out = sem("m_pe"), sem("m_out")
        hid_raw, hid_mm, hid_th, hid_done, pc_s, pc_e = (sem(n) for n in ("hid_raw", "hid_mm", "hid_th", "hid_done", "pc_s", "pc_e"))
        l_mm, s_done, e_done, p_done, t_mm, t_out, v_mm, v_out = (sem(n) for n in (
            "l_mm", "s_done", "e_done", "p_done", "t_mm", "t_out", "v_mm", "v_out"))
        ya_hi_done, ya_lo_done, yb_hi_done, yb_lo_done = (sem(n) for n in ("ya_hi_done", "ya_lo_done", "yb_hi_done", "yb_lo_done"))
        mg_done, pa_done, pb_read, mix_done, mix_hi_done, mix_lo_done = (sem(n) for n in (
            "mg_done", "pa_done", "pb_read", "mix_done", "mix_hi_done", "mix_lo_done"))
        x1_done, sg_done, gu_done, g_hi_done, g_lo_done, fin = (sem(n) for n in (
            "x1_done", "sg_done", "gu_done", "g_hi_done", "g_lo_done", "fin"))

        def wait_bank(eng, n):
            if n not in BANK_USE or BANK_USE[n] < 2:
                return
            m = BANK_USER[BANK_USE[n] - 2]
            kind, i = CHUNKS[m]
            if kind in COPIED:
                eng.wait_ge(copied, COPY_NO[m] + 1)
            elif kind in ("mga", "mgb"):
                eng.wait_ge(mg_done, i + 1 + (4 if kind == "mgb" else 0))
            else:
                eng.wait_ge({"gz": zs_done, "pa": pa_done, "pb": pb_read, "wo": x1_done, "gu": gu_done}[kind], i + 1)

        def chunk_source(n):
            kind, i = CHUNKS[n]
            wide = lambda w, c: w.rearrange("(k p) n -> p k n", p=P)[:, :, c:c + CW]
            first = {"gk": GK, "gq": GQ, "gv": GV, "gz": GZ, "nq": NQ, "kc": NKV, "vc": NKV + KV_W, "ks": NKV + 2 * KV_W,
                     "vs": NKV + 3 * KV_W, "kw": NKV + 4 * KV_W, "vw": NKV + 5 * KV_W, "mga": MGATE, "mgb": MGATE + D_MODEL}
            if kind in first:
                return [(slice(0, CW), wide(w_in[0], first[kind] + i * CW))]
            if kind in ("pa", "pb", "wo"):
                return [(slice(0, CW), wide({"pa": w_proj_a, "pb": w_proj_b, "wo": w_out}[kind][0], i * CW))]
            if kind in ("cmpk", "cmpv"):
                w = cmp_w1[0, 0 if kind == "cmpk" else 1].rearrange("(j p) n -> p j n", p=P)
                return [(slice(0, CW), w[:, i * KT:(i + 1) * KT, :])]
            if kind == "gu":
                return [(slice(0, P), w_gate[0].rearrange("(k p) n -> p k n", p=P)[:, :, i * P:(i + 1) * P]),
                        (slice(P, CW), w_up[0].rearrange("(k p) n -> p k n", p=P)[:, :, i * P:(i + 1) * P])]
            return [(None, w_down[0].rearrange("(k p) n -> p k n", p=P)[:, 2 * i:2 * i + 2, :])]

        def tap(k, a, j):
            tile_no = {0: 8, 1: 0, 2: 16}[k // 4] + 2 * (k % 4) + a
            return cols_a[:, j * 24 + tile_no:j * 24 + tile_no + 1]

        def loads_before(n):
            return sum(len(chunk_source(m)) for m in range(n % NRAW, n + 1, NRAW))

        def wait_use(eng, name, b):
            u = stage_use(name, b)
            eng.wait_ge(g_out[u % GRING], u // GRING + 1)

        def level_columns(name):
            return {f"X{LEVELS - 1}": slice(0, P // 2), f"Z{LEVELS - 1}": slice(P // 2, P)}.get(name, slice(0, P))

        def problems(t, b):
            return t[:, 4 * b:4 * b + 4, :]

        def pcol(name, b):
            return col[name][:, 2 * b:2 * b + 2, :].rearrange("p h t -> p (h t)")

        def wide_col(name, b):
            return pcol(name, b).unsqueeze(2).to_broadcast([P, 4, P])

        block = ctx.enter_context(nc.Block())

        @block.sync
        def _(sp):
            sp.dma_start(x_sb[:], x[0].rearrange("(t p) d -> p t d", p=P)).then_inc(x_in, 16)
            sp.dma_start(ident[:], c_ident).then_inc(ident_in, 16)

            def load_chunk(n):
                if n >= NRAW:
                    sp.wait_ge(hi_done, n - NRAW + 1)
                    sp.wait_ge(lo_done, n - NRAW + 1)
                for where, src in chunk_source(n):
                    r = raw[n % NRAW]
                    dst = r[:, :, where] if where is not None else r[:].rearrange("p k c -> p (k c)").rearrange("p (k c) -> p k c", k=2)
                    sp.dma_start(dst, src).then_inc(raw_in[n % NRAW], 16)

            load_chunk(0)
            sp.wait_ge(vec_in, 112)
            for n in range(1, len(CHUNKS)):
                load_chunk(n)
            for i in range(4):
                sp.wait_ge(fin, i + 1)
                t, c = i // 2, i % 2
                sp.dma_start(out[0].rearrange("(t p) d -> p t d", p=P)[:, t, c * 512:(c + 1) * 512],
                             out_sb[:, t, c * 512:(c + 1) * 512]).then_inc(out_done, 16)
            sp.wait_ge(out_done, 64)

        @block.gpsimd
        def _(pool):
            nc.gpsimd.memset(ones[:], 1.0).then_inc(ones_set, 1)
            nc.gpsimd.memset(ones_sq[:], 1.0).then_inc(ones_set, 1)
            nc.gpsimd.memset(relb[:], 1.0).then_inc(relb_set, 1)
            pool.wait_ge(relb_set, 1)
            pool.dma_start(relb[0:REL_BUCKETS, :], rel_bias).then_inc(misc_in, 16)
            pool.dma_start(onehot[:], c_onehot).then_inc(misc_in, 16)
            pool.dma_start(cmp2[:], cmp_w2[0].rearrange("c (k p) d -> p c k d", p=P)).then_inc(misc_in, 16)
            pool.dma_start(rowvalid[:], c_rowvalid).then_inc(misc_in, 16)
            pool.dma_start(par[:, 0, :], a_log[0:1, :].to_broadcast([P, HEADS])).then_inc(misc_in, 16)
            pool.dma_start(par[:, 1, :], dt_bias[0:1, :].to_broadcast([P, HEADS])).then_inc(misc_in, 16)
            pool.dma_start(flip[:], c_flip).then_inc(bias_in, 16)
            pool.wait_ge(pre_dve, 4)
            pool.dma_start(bias_rows, bias_v[:]).then_inc(bias_out, 16)
            pool.wait_ge(bias_out, 16)
            pool.dma_start(bias_up[:], bass.AP(bias_rows.tensor, 0, [[1, P], [384, HEADS], [1, SEQ]])).then_inc(bias_in, 16)
            pool.dma_start(levels[:], c_levels).then_inc(levels_in, 16)
            pool.wait_ge(conv_done, 12)
            pool.wait_ge(colsum, 8)
            pool.wait_ge(ident_in, 16)
            nc.gpsimd.tensor_copy(Db[:], ident[:].unsqueeze(1).to_broadcast([P, 16, P])).then_inc(d_init, 1)
            nc.gpsimd.tensor_copy(DTb[:], ident[:].unsqueeze(1).to_broadcast([P, 16, P])).then_inc(d_init, 1)
            for b in range(NB):
                pool.wait_ge(g_mm, stage_use("knT", b) + 1)
                nc.gpsimd.tensor_tensor(problems(kn, b), problems(kn, b), wide_col("kf", b), ALU.mult).then_inc(kf_ready, 1)
            for b in range(NB):
                pool.wait_ge(of_ready, 1)
                nc.gpsimd.tensor_tensor(problems(kT, b), problems(kT, b), wide_col("of", b), ALU.mult).then_inc(on_ready, 1)

        @block.scalar
        def _(act):
            count = [0]

            def link(ins):
                count[0] += 1
                ins.then_inc(act_step, 1)
                act.wait_ge(act_step, count[0])

            act.dma_start(rows_a[:], conv_w[0].rearrange("j (c p) -> (j c) p", p=P)).then_inc(vec_in, 16)
            act.dma_start(rows_b[ROW_N1:ROW_N1 + KT, :], norm1_w[0].rearrange("(k p) -> k p", p=P)).then_inc(vec_in, 16)
            act.dma_start(rows_b[ROW_N2:ROW_N2 + KT, :], norm2_w[0].rearrange("(k p) -> k p", p=P)).then_inc(vec_in, 16)
            act.dma_start(rows_b[ROW_GDN:ROW_GDN + 1, :], gdn_norm_w).then_inc(vec_in, 16)
            act.dma_start(rows_b[ROW_QN:ROW_QN + 1, :], q_norm_w).then_inc(vec_in, 16)
            act.dma_start(rows_b[ROW_KN:ROW_KN + 3, :], k_norm_w[0]).then_inc(vec_in, 16)
            act.dma_start(rows_b[ROW_PE:NROWS, :], cmp_pe[0].rearrange("c j d -> (c j) d")).then_inc(vec_in, 16)
            wi = w_in[0].rearrange("(k p) n -> p k n", p=P)
            act.dma_start(wsm[:, :, 0:2 * HEADS], wi[:, :, GA:GA + 2 * HEADS]).then_inc(small_in, 16)
            act.dma_start(wsm[:, :, 2 * HEADS:], wi[:, :, NGATE:NGATE + 3 * HEADS]).then_inc(small_in, 16)
            act.dma_start(upper[:], c_upper).then_inc(const_in, 16)
            act.dma_start(negmask[:], c_negmask).then_inc(const_in, 16)

            def split_hi(n):
                act.wait_ge(raw_in[n % NRAW], 16 * loads_before(n))
                if n >= NSPL:
                    act.wait_ge(half_done, 2 * (n - NSPL) + 2)
                nc.scalar.activation(w_hi[n % NSPL][:], raw[n % NRAW][:], ACT.Copy).then_inc(hi_done, 1)

            act.wait_ge(x_in, 16)
            for t in range(TT):
                nc.scalar.activation(xn_sb[:, t, :], x_sb[:, t, :], ACT.Square, accum_out=scol["x"][:, t:t + 1]).then_inc(xss, 1)
            split_hi(0)
            act.wait_ge(small_in, 32)
            nc.scalar.activation(wsm_hi[:], wsm[:], ACT.Copy).then_inc(pre_act, 1)
            for k in range(KT):
                act.wait_ge(tr_ready, k // 2 + 1)
                if k == 0:
                    act.wait_ge(pre_dve, 2)
                nc.scalar.activation(h_hi[:, k, :], ps[2 + k // 2][:, (k % 2) * SEQ:(k % 2 + 1) * SEQ], ACT.Copy,
                                     scale=cols_b[:, ROW_N1 + k:ROW_N1 + k + 1]).then_inc(h_hi_done, 1)

            act.wait_ge(pre_pe, 4)
            nc.scalar.activation(small_ch[:], ps[1][0:NSMALL, 0:SEQ], ACT.Copy).then_inc(small_raw, 1)

            def small_gates():
                act.wait_ge(cols_ready, 1)
                link(nc.scalar.activation(col["t0"][:], col["t0"][:], ACT.Exp))
                link(nc.scalar.activation(col["t0"][:], col["t0"][:], ACT.Ln, bias=ones[:, 0:1]))
                act.wait_ge(misc_in, 96)
                nc.scalar.activation(par[:, 0, :], par[:, 0, :], ACT.Exp)
                nc.scalar.activation(col["beta"][:], small[:, :, HEADS:2 * HEADS].rearrange("p t h -> p h t"), ACT.Tanh, scale=0.5)
                nc.scalar.activation(gates[:], small[:, :, 2 * HEADS:], ACT.Tanh, scale=0.5).then_inc(pre_act, 1)

            def decay_factors():
                act.wait_ge(cols_ready, 2)
                nc.scalar.activation(col["eg"][:], col["gc"][:], ACT.Exp)
                nc.scalar.activation(col["kf"][:], col["gl"][:], ACT.Exp).then_inc(pre_act, 1)

            def evacuate(n):
                kind, i = CHUNKS[n]
                if n not in BANK_USE:
                    return
                u = BANK_USE[n]
                bank = stream_ps[u % 2][:].rearrange("p (a c) -> p a c", a=2)
                act.wait_ge(half_done, 2 * n + 2)
                if kind in ("gk", "gq", "gv"):
                    k = {"gk": 0, "gq": 4, "gv": 8}[kind] + i
                    if k >= 2:
                        act.wait_ge(conv_done, k - 1)
                    else:
                        act.wait_ge(pre_dve, 1)
                    nc.scalar.activation(cin[k % 2][:, :, CONV - 1:CONV - 1 + SEQ], bank, ACT.Copy)
                    for a in range(2):
                        ins = nc.scalar.activation(cacc[k % 2][:, a, :], bank[:, a, :], ACT.Copy, scale=tap(k, a, CONV - 1))
                    ins.then_inc(copied, 1)
                elif kind == "gz":
                    if i == 0:
                        act.wait_ge(colsum, 12)
                    else:
                        act.wait_ge(zs_done, i)
                    nc.scalar.activation(gate_t[:], bank, ACT.Tanh, scale=0.5).then_inc(zt, 1)
                elif kind == "nq":
                    nc.scalar.activation(nqT[:, 2 * i:2 * i + 2, :], bank, ACT.Copy).then_inc(copied, 1)
                    act.wait_ge(copied, COPY_NO[n] + 1)
                    if i >= 1:
                        act.wait_ge(colsum, 8 + i)
                    nc.scalar.activation(nsq[:], nqT[:, 2 * i:2 * i + 2, :], ACT.Square).then_inc(nq_sq, 1)
                elif kind in ("ks", "kw"):
                    j = 0 if kind == "ks" else 1
                    nc.scalar.activation(key_tok[:, j, :, :].rearrange("p a d -> p (a d)"), stream_ps[u % 2][:], ACT.Copy).then_inc(copied, 1)
                    act.wait_ge(copied, COPY_NO[n] + 1)
                    for q in range(4):
                        nc.scalar.activation(sc[j][:].rearrange("p a c -> p (a c)")[:, q * DH:(q + 1) * DH], key_tok[:, j, q, :], ACT.Square,
                                             accum_out=ksum[:, 4 * j + q:4 * j + q + 1]).then_inc(key_in, 1)
                elif kind in ("vs", "vw"):
                    dst = vs if kind == "vs" else vw
                    nc.scalar.activation(dst[:].rearrange("p t g d -> p (t g d)"), stream_ps[u % 2][:], ACT.Copy).then_inc(copied, 1)
                elif kind in ("kc", "vc"):
                    j = 0 if kind == "kc" else 1
                    nc.scalar.activation(cmp_raw[:, j, :, :], bank, ACT.Copy).then_inc(copied, 1)
                elif kind in ("mga", "mgb"):
                    j = i + (4 if kind == "mgb" else 0)
                    if kind == "mga" and i != 1:
                        act.wait_ge(pa_done if i else zs_done, i - 1 if i else 4)
                    elif kind == "mgb":
                        act.wait_ge(pb_read if i >= 2 else pa_done, i - 1 if i >= 2 else 3 + i)
                    nc.scalar.activation(gates_t[i % 2][:], bank, ACT.Tanh, scale=0.5).then_inc(mg_done, 1)
                elif kind == "gu":
                    if i >= 2:
                        act.wait_ge(gu_done, i - 1)
                    nc.scalar.activation(sg[i % 2][:], bank[:, 0, :], ACT.Silu).then_inc(sg_done, 1)

            def evacuate_late(n):
                kind, i = CHUNKS[n]
                if kind == "wo":
                    act.wait_ge(x1_done, i + 1)
                    for t in range(TT):
                        c = slice(i * CW, (i + 1) * CW)
                        nc.scalar.activation(x1n[:, t, c], x1[:, t, c], ACT.Square, accum_out=xs[:, t, i:i + 1]).then_inc(xss, 1)
                elif kind == "pb":
                    act.wait_ge(mix_done, i + 1)
                    nc.scalar.activation(mix_hi[:, 2 * i:2 * i + 2, :], mix[:, 2 * i:2 * i + 2, :], ACT.Copy, scale=0.5).then_inc(mix_hi_done, 1)
                elif kind == "gu":
                    act.wait_ge(gu_done, i + 1)
                    if i >= 4:
                        act.wait_ge(half_done, 2 * AT["dn", (i - 4) // 2] + 1 + i % 2)
                    nc.scalar.activation(g_hi[i % 4][:], gu[i % 2][:], ACT.Copy).then_inc(g_hi_done, 1)

            def conv_step(k, part):
                if part == 0:
                    act.wait_ge(conv_acc, k + 1)
                    nc.scalar.activation(cth[k % 2][:], cacc[k % 2][:], ACT.Tanh, scale=0.5).then_inc(conv_th, 1)
                elif k < 8:
                    act.wait_ge(conv_done, k + 1)
                    if k >= 2:
                        act.wait_ge(colsum, k - 1)
                    src = (kT if k < 4 else qT)[:, 4 * (2 * (k % 4)) // 2:4 * (2 * (k % 4)) // 2 + 4, :]
                    nc.scalar.activation(csq[k % 2][:].rearrange("p a (t c) -> p (a t) c", t=TT), src, ACT.Square).then_inc(conv_sq, 1)

            def gdn(name):
                for b in range(NB):
                    u = stage_use(name, b)
                    bank, done = gdn_ps[u % GRING], g_out[u % GRING]
                    b4 = bank[:].rearrange("p (q c) -> p q c", q=4)
                    if name == "row":
                        act.wait_ge(done, u // GRING + 1)
                        nc.scalar.activation(problems(ET, b), problems(ET, b), ACT.Exp).then_inc(et_ready, 1)
                    elif name in ("knT", "at") or name[0] == "X":
                        dst = {"k": kT, "a": ATb, "X": AXb}[name[0]]
                        act.wait_ge(g_mm, u + 1)
                        if name == "X1":
                            act.wait_ge(lvl0, b + 1)
                        c = level_columns(name)
                        nc.scalar.activation(problems(dst, b)[:, :, c], b4[:, :, c], ACT.Copy).then_inc(done, 1)
                    elif name == "w0":
                        act.wait_ge(g_mm, u + 1)
                        link(nc.scalar.activation(problems(AXb, b)[:, 0:4:2, :], b4[:, 0:2, :], ACT.Copy))
                        nc.scalar.activation(problems(Db, b)[:, 1:4:2, :], b4[:, 2:4, :], ACT.Copy, scale=-1.0).then_inc(done, 1)
                    elif name == "v1":
                        act.wait_ge(g_mm, u + 1)
                        link(nc.scalar.activation(problems(AXb, b)[:, 1:4:2, :], b4[:, 0:2, :], ACT.Copy))
                        for hh in range(2):
                            h = 2 * b + hh
                            ins = nc.scalar.activation(problems(Db, b)[:, 2 * hh + 1, :], b4[:, 2 + hh, :], ACT.Copy,
                                                       scale=col["eg"][:, h, 1:2])
                            if hh == 0:
                                link(ins)
                            else:
                                ins.then_inc(done, 1)
                    elif name == "o1":
                        act.wait_ge(o_ready, b + 1)
                        for q in range(4):
                            ins = nc.scalar.activation(problems(kn, b)[:, q, :], problems(kT, b)[:, q, :], ACT.Square,
                                                       accum_out=pcol("ss", b)[:, q:q + 1]).then_inc(ss_ready, 1)

            def misc(m):
                if m in (TURN_KS, TURN_KW):
                    act.wait_ge(m_pe, m + 1)
                    j = m - TURN_KS
                    dst = (ksT, kwT)[j][:].rearrange("p g (t c) -> p t g c", t=TT)
                    nc.scalar.activation(dst, log_ps[:].rearrange("p (t g c) -> p t g c", t=TT, g=GROUPS), ACT.Copy,
                                         scale=wk[:, 1 + j:2 + j]).then_inc(m_out, 1)
                elif m == TURN_KC:
                    act.wait_ge(m_pe, m + 1)
                    nc.scalar.activation(kcT[:, :, 0:NCMP], log_ps[:, 0:32].rearrange("p (g c) -> p g c", g=GROUPS)[:, :, 0:NCMP],
                                         ACT.Copy, scale=wk[:, 0:1]).then_inc(m_out, 1)
                elif m == W2_V:
                    act.wait_ge(m_pe, m + 1)
                    nc.scalar.activation(vc[:].rearrange("p g d -> p (g d)"), log_ps[0:NCMP, 0:GROUPS * DH], ACT.Copy).then_inc(m_out, 1)
                elif m == LOGITS_C:
                    act.wait_ge(pc_s, 1)
                    nc.scalar.activation(pc[:], pc[:], ACT.Exp).then_inc(pc_e, 1)
                elif m >= TURN_PC:
                    act.wait_ge(m_pe, m + 1)
                    q = 4 * (m - TURN_PC)
                    nc.scalar.activation(pcT[:, q:q + 4, :], log_ps[0:NCMP, :].rearrange("p (a c) -> p a c", a=4), ACT.Copy).then_inc(m_out, 1)

            def hidden(c):
                act.wait_ge(hid_mm, c + 1)
                nc.scalar.activation(hid[:, c, :, :].rearrange("p a m -> p (a m)"), ps[7][:, 0:64], ACT.Tanh, scale=0.5).then_inc(hid_th, 1)

            def unit(i):
                if i < len(UNITS):
                    h, t = UNITS[i]
                    w = P * (t + 1)
                    act.wait_ge(s_done, i + 1)
                    for a in range(2):
                        nc.scalar.activation(sc[i % 3][:, a, 0:w], sc[i % 3][:, a, 0:w], ACT.Exp,
                                             bias=scol["nm"][:, 2 * (i % 3) + a:2 * (i % 3) + a + 1],
                                             accum_out=scol["se"][:, 2 * (i % 3) + a:2 * (i % 3) + a + 1]).then_inc(e_done, 1)
                if 2 <= i < len(UNITS) + 2:
                    j = i - 2
                    h, t = UNITS[j]
                    act.wait_ge(t_mm, j + 1)
                    if j >= 2:
                        act.wait_ge(v_mm, j - 1)
                    nb = 2 * (t + 1)
                    nc.scalar.activation(pt[j % 2][:, 0:nb, :], pt_ps[:].rearrange("p (a c) -> p a c", a=4)[:, 0:nb, :], ACT.Copy).then_inc(t_out, 1)
                if i >= 3:
                    j = i - 3
                    h, t = UNITS[j]
                    act.wait_ge(v_mm, j + 1)
                    nc.scalar.activation(nqT[:, h, t * P:(t + 1) * P], pv_ps[:, 0:P], ACT.Copy).then_inc(v_out, 1)

            def second_norm():
                for k in range(KT):
                    act.wait_ge(tr_ready, 4 + k // 2 + 1)
                    nc.scalar.activation(h_hi[:, k, :], ps[2 + k // 2][:, (k % 2) * SEQ:(k % 2 + 1) * SEQ], ACT.Copy,
                                         scale=cols_b[:, ROW_N2 + k:ROW_N2 + k + 1]).then_inc(h_hi_done, 1)

            for n in range(len(CHUNKS) + 1):
                kind, i = CHUNKS[n] if n < len(CHUNKS) else (None, 0)
                if n == 0:
                    split_hi(1)
                    small_gates()
                else:
                    conv_phase = n <= FIRST_STAGE_SLOT
                    if not conv_phase:
                        evacuate(n - 1)
                    if CHUNKS[n - 1] in LAST_OF_KIND:
                        evacuate_late(n - 1)
                    if n == AT["gu", 0]:
                        second_norm()
                    if n + 1 < len(CHUNKS):
                        split_hi(n + 1)
                    if conv_phase:
                        evacuate(n - 1)
                    if CHUNKS[n - 1] not in LAST_OF_KIND:
                        evacuate_late(n - 1)
                if n == 1:
                    decay_factors()
                for k in {FIRST_STAGE_SLOT: [n - 2, n - 1]}.get(n, [n - 2] if 2 <= n < FIRST_STAGE_SLOT else []):
                    conv_step(k, 0)
                    conv_step(k, 1)
                if n == AT["mga", 1]:
                    act.wait_ge(zs_done, 4 + NB)
                    for b in range(NB):
                        nc.scalar.activation(ya_hi[:, 2 * b:2 * b + 2, :], zsT[:, 2 * b:2 * b + 2, :], ACT.Copy).then_inc(ya_hi_done, 1)
                for half in range(2):
                    for name in slot_stages(n, half):
                        gdn(name)
                    if n - 1 in (AT["cmpk", 3], AT["cmpv", 3]):
                        c = 0 if n - 1 == AT["cmpk", 3] else 1
                        if half == 0:
                            act.wait_ge(half_done, 2 * n)
                            nc.scalar.activation(hid_tok[:], ps[6][0:32, 0:CW], ACT.Copy).then_inc(hid_raw, 1)
                        else:
                            hidden(c)
                    for m in slot_misc(n, half):
                        misc(m)
                    for i in slot_units(n, half):
                        unit(i)
                if n == AT["pa", 0]:
                    act.wait_ge(g_mm, NB * len(STAGES))
                    act.dma_start(x1[:], x[0].rearrange("(t p) d -> p t d", p=P)).then_inc(xres_in, 16)
                if n == AT["mgb", 0]:
                    act.wait_ge(v_out, len(UNITS))
                    for b in range(NB):
                        nc.scalar.activation(yb_hi[:, 2 * b:2 * b + 2, :], nqT[:, 2 * b:2 * b + 2, :], ACT.Copy).then_inc(yb_hi_done, 1)

        @block.vector
        def _(dve):
            count = [0]

            def link(ins):
                count[0] += 1
                ins.then_inc(dve_step, 1)
                dve.wait_ge(dve_step, count[0])

            def split_lo(n):
                dve.wait_ge(raw_in[n % NRAW], 16 * loads_before(n))
                dve.wait_ge(hi_done, n + 1)
                nc.vector.tensor_tensor(w_lo[n % NSPL][:], raw[n % NRAW][:], w_hi[n % NSPL][:].bitcast(f32),
                                        ALU.subtract).then_inc(lo_done, 1)

            def rsqrt(y, xx, u, done=None):
                link(nc.vector.tensor_scalar(u.bitcast(i32), xx.bitcast(i32), 1, None, ALU.logical_shift_right))
                link(nc.vector.tensor_scalar(y.bitcast(i32), u.bitcast(i32), -1, 0x5F3759DF, ALU.mult, ALU.add))
                for k in range(3):
                    link(nc.vector.tensor_tensor(u, y, y, ALU.mult))
                    link(nc.vector.scalar_tensor_tensor(u, u, -0.5, xx, ALU.mult, ALU.mult))
                    last = nc.vector.scalar_tensor_tensor(y, u, 1.5, y, ALU.add, ALU.mult)
                    if done is None or k < 2:
                        link(last)
                    else:
                        last.then_inc(done, 1)

            def normalise(src, dst, norms_before):
                dve.wait_ge(xss, norms_before + TT)
                link(nc.vector.tensor_scalar(scol["x"][:, 2:4], scol["x"][:, 0:2], 1.0 / D_MODEL, EPS, ALU.mult, ALU.add))
                rsqrt(scol["x"][:, 4:6], scol["x"][:, 2:4], scol["x"][:, 6:8])
                for t in range(TT):
                    nc.vector.tensor_scalar(dst[:, t, :], src[:, t, :], scol["x"][:, 4 + t:5 + t], None, ALU.mult).then_inc(xn_done, 1)

            def h_low(before, row):
                for k in range(KT):
                    dve.wait_ge(h_hi_done, before + 2 * (k // 2) + 2)
                    nc.vector.scalar_tensor_tensor(h_lo[:, k, :], ps[2 + k // 2][:, (k % 2) * SEQ:(k % 2 + 1) * SEQ],
                                                   cols_b[:, row + k:row + k + 1], h_hi[:, k, :].bitcast(f32),
                                                   ALU.mult, ALU.subtract).then_inc(h_lo_done, 1)

            nc.vector.memset(cin[0][:, :, 0:3], 0.0)
            nc.vector.memset(cin[1][:, :, 0:3], 0.0).then_inc(pre_dve, 1)
            normalise(x_sb, xn_sb, 0)
            dve.wait_ge(pre_pe, 2)
            link(nc.vector.tensor_copy(cols_a[:], ps[7][:, 0:CONV * 24]))
            nc.vector.tensor_copy(cols_b[:], ps[7][:, P:P + NROWS]).then_inc(pre_dve, 1)
            dve.wait_ge(pre_dve, 2)
            link(nc.vector.tensor_scalar(wk[:], cols_b[:, ROW_KN:ROW_KN + 3], cols_b[:, ROW_QN:ROW_QN + 1], DH ** -0.5, ALU.mult, ALU.mult))
            link(nc.vector.tensor_scalar(zw[:], cols_b[:, ROW_GDN:ROW_GDN + 1], 0.5, None, ALU.mult))
            split_lo(0)
            dve.wait_ge(pre_act, 1)
            nc.vector.tensor_tensor(wsm_lo[:], wsm[:], wsm_hi[:].bitcast(f32), ALU.subtract).then_inc(pre_dve, 1)
            h_low(0, ROW_N1)
            dve.wait_ge(pre_pe, 3)
            nc.vector.tensor_copy(bias_v[:], ps[6][0:HEADS, 0:384]).then_inc(pre_dve, 1)

            def small_gates():
                dve.wait_ge(small_mm, 1)
                link(nc.vector.tensor_copy(small[:].rearrange("p t c -> p (t c)"), ps[7][:, 256:256 + TT * NSMALL]))
                dve.wait_ge(misc_in, 96)
                a = small[:, :, 0:HEADS].rearrange("p t h -> p h t")
                link(nc.vector.tensor_tensor(col["t1"][:], a, par[:, 1, :].unsqueeze(2).to_broadcast([P, HEADS, TT]), ALU.add))
                link(nc.vector.tensor_scalar(col["t2"][:], col["t1"][:], -1.0, None, ALU.mult))
                nc.vector.tensor_tensor(col["t0"][:], col["t1"][:], col["t2"][:], ALU.min).then_inc(cols_ready, 1)
                link(nc.vector.tensor_scalar(col["t1"][:], col["t1"][:], 0.0, None, ALU.max))
                dve.wait_ge(pre_act, 2)
                link(nc.vector.tensor_tensor(col["t1"][:], col["t1"][:], col["t0"][:], ALU.add))
                link(nc.vector.scalar_tensor_tensor(col["g"][:], col["t1"][:], -1.0, par[:, 0, :].unsqueeze(2).to_broadcast([P, HEADS, TT]), ALU.mult, ALU.mult))
                link(nc.vector.tensor_scalar(col["beta"][:], col["beta"][:], 0.5, 0.5, ALU.mult, ALU.add))
                nc.vector.tensor_scalar(col["hbeta"][:], col["beta"][:], 0.5, None, ALU.mult)
                nc.vector.tensor_scalar(col["nbeta"][:], col["beta"][:], -1.0, None, ALU.mult)
                nc.vector.tensor_scalar(gates[:], gates[:], 0.5, 0.5, ALU.mult, ALU.add).then_inc(pre_dve, 1)

            def decay_factors():
                dve.wait_ge(pre_pe, 5)
                link(nc.vector.tensor_copy(col["gc"][:].rearrange("p h t -> p (h t)"), ps[7][:, 384:400]))
                nc.vector.tensor_tensor(col["gl"][:].rearrange("p h t -> p (h t)"), ps[7][:, 400:416],
                                        col["gc"][:].rearrange("p h t -> p (h t)"), ALU.subtract).then_inc(cols_ready, 1)
                dve.wait_ge(pre_act, 3)
                link(nc.vector.tensor_tensor(col["kf"][:, :, 1], col["beta"][:, :, 1], col["eg"][:, :, 1], ALU.mult))

            def conv(k):
                dve.wait_ge(copied, k + 1)
                step = [0, 0]
                for j in range(CONV - 1):
                    for a in range(2):
                        acc, src = cacc[k % 2][:, a, :], cin[k % 2]
                        if j:
                            dve.wait_ge(dve_step, step[a])
                        ins = nc.vector.scalar_tensor_tensor(acc, src[:, a, j:j + SEQ], tap(k, a, j), acc, ALU.mult, ALU.add)
                        if (j, a) == (CONV - 2, 1):
                            ins.then_inc(conv_acc, 1)
                        else:
                            count[0] += 1
                            step[a] = count[0]
                            ins.then_inc(dve_step, 1)

            def conv_finish(k):
                dve.wait_ge(conv_th, k + 1)
                dst = (kT, qT, vT)[k // 4][:, 4 * (k % 4):4 * (k % 4) + 4, :]
                v = lambda t: t[:].rearrange("p a (t c) -> p (a t) c", t=TT)
                nc.vector.scalar_tensor_tensor(dst, v(cth[k % 2]), 1.0, v(cacc[k % 2]), ALU.add, ALU.mult).then_inc(conv_done, 1)

            def inverse_norm(name, bank, scale, eps, after):
                f = lambda n: col[n][:].rearrange("p h t -> p (h t)")
                link(nc.vector.tensor_scalar(f("t1"), bank[:, 0:16], scale, eps, ALU.mult, ALU.add))
                rsqrt(f(name), f("t1"), f("t2"))
                return nc.vector.tensor_scalar(f(name), f(name), after, None, ALU.mult)

            def gdn(name):
                for b in range(NB):
                    u = stage_use(name, b)
                    bank, done = gdn_ps[u % GRING], g_out[u % GRING]
                    b4 = bank[:].rearrange("p (q c) -> p q c", q=4)
                    mine = name in ("row", "kt", "vt", "gram", "kq", "m1t", "s1", "o1", "ot") or name[0] in "YZ"
                    if mine:
                        dve.wait_ge(g_mm, u + 1)
                    if name == "row":
                        for q in range(4):
                            ins = nc.vector.scalar_tensor_tensor(problems(ET, b)[:, q, :], b4[:, q, :], pcol("gc", b)[:, q:q + 1],
                                                                 negmask[:], ALU.subtract, ALU.add)
                        ins.then_inc(done, 1)
                    elif name == "kt":
                        nc.vector.tensor_tensor(problems(kn, b), b4, wide_col("rk", b), ALU.mult).then_inc(done, 1)
                    elif name == "vt":
                        nc.vector.tensor_tensor(problems(vT, b), b4, wide_col("hbeta", b), ALU.mult).then_inc(done, 1)
                    elif name == "gram":
                        dve.wait_ge(et_ready, b + 1)
                        nc.vector.tensor_tensor(problems(AXb, b), b4, problems(ET, b), ALU.mult).then_inc(done, 1)
                    elif name == "kq":
                        nc.vector.tensor_tensor(problems(ET, b), b4, problems(ET, b), ALU.mult).then_inc(done, 1)
                    elif name == "m1t":
                        nc.vector.tensor_tensor(problems(AXb, b), b4, wide_col("nbeta", b), ALU.mult).then_inc(done, 1)
                    elif name == "at":
                        wait_use(dve, "at", b)
                        if b == 0:
                            dve.wait_ge(d_init, 2)
                            dve.wait_ge(levels_in, 16)
                        m = lambda l: levels[:, l, :].unsqueeze(1).to_broadcast([P, 4, P])
                        nc.vector.copy_predicated(problems(Db, b), m(0), problems(AXb, b))
                        nc.vector.copy_predicated(problems(DTb, b), m(LEVELS), problems(ATb, b)).then_inc(lvl0, 1)
                    elif name[0] in "YZ":
                        l = int(name[1:])
                        c = level_columns(name)
                        m = levels[:, l + (LEVELS if name[0] == "Z" else 0), c].unsqueeze(1).to_broadcast([P, 4, c.stop - c.start])
                        nc.vector.copy_predicated(problems(Db if name[0] == "Y" else DTb, b)[:, :, c], m, b4[:, :, c]).then_inc(done, 1)
                    elif name == "s1":
                        link(nc.vector.tensor_copy(problems(Db, b)[:, 0:4:2, :], b4[:, 0:2, :]))
                        nc.vector.tensor_tensor(problems(kT, b)[:, 0:4:2, :], b4[:, 2:4, :],
                                                pcol("rq", b)[:, 0:4:2].unsqueeze(2).to_broadcast([P, 2, P]), ALU.mult).then_inc(done, 1)
                    elif name == "o1":
                        nc.vector.tensor_tensor(problems(kT, b)[:, 1:4:2, :], b4[:, 0:2, :], problems(Db, b)[:, 1:4:2, :],
                                                ALU.add).then_inc(done, 1)
                        wait_use(dve, "o1", b)
                        nc.vector.tensor_tensor(problems(kT, b)[:, 1:4:2, :], problems(kT, b)[:, 1:4:2, :],
                                                pcol("rq", b)[:, 1:4:2].unsqueeze(2).to_broadcast([P, 2, P]), ALU.mult).then_inc(o_ready, 1)
                        if b == NB - 1:
                            dve.wait_ge(ss_ready, 4 * NB)
                            f = lambda n: col[n][:].rearrange("p h t -> p (h t)")
                            link(nc.vector.tensor_scalar(f("t1"), f("ss"), 1.0 / DH, EPS, ALU.mult, ALU.add))
                            rsqrt(f("of"), f("t1"), f("t2"), of_ready)
                    elif name == "ot":
                        dve.wait_ge(zs_done, 4)
                        z = zsT[:, 2 * b:2 * b + 2, :].rearrange("p h (t c) -> p (h t) c", t=TT)
                        nc.vector.scalar_tensor_tensor(z, b4, zw[:], z, ALU.mult, ALU.mult).then_inc(zs_done, 1)

            def keys(j):
                dve.wait_ge(key_in, 4 * j + 4)
                link(nc.vector.tensor_scalar(kr[:, 4 * j:4 * j + 4], ksum[:, 4 * j:4 * j + 4], 1.0 / DH, EPS, ALU.mult, ALU.add))
                rsqrt(scol["c"][:, 4 * j:4 * j + 4], kr[:, 4 * j:4 * j + 4], scol["d"][:, 0:4])
                nc.vector.tensor_tensor(key_tok[:, j, :, :], key_tok[:, j, :, :],
                                        scol["c"][:, 4 * j:4 * j + 4].unsqueeze(2).to_broadcast([P, 4, DH]), ALU.mult).then_inc(key_n, 1)

            def flatten(c):
                dve.wait_ge(copied, COPY_NO[AT["kc" if c == 0 else "vc", 0]] + 1)
                if c == 1:
                    dve.wait_ge(half_done, 2 * AT["cmpk", 3] + 2)
                link(nc.vector.memset(sc[0][:].rearrange("p a c -> p (a c)"), 0.0))
                for r in range(2):
                    s = sc[0][:].rearrange("p a c -> p (a c)").rearrange("p (j g n) -> p j g n", j=16, g=GROUPS)
                    for g in range(GROUPS):
                        src = cmp_raw[:, c, g, :].rearrange("p (n j) -> p j n", j=CMP_STRIDE)[:, :, r:r + NCMP]
                        e = cols_b[:, ROW_PE + c * CMP_BLOCK + r * 16:ROW_PE + c * CMP_BLOCK + (r + 1) * 16]
                        link(nc.vector.tensor_tensor(s[:, :, g, 0:NCMP], src, e.unsqueeze(2).to_broadcast([P, 16, NCMP]), ALU.add))
                    sf = sc[0][:].rearrange("p a c -> p (a c)").rearrange("p (j m) -> p j m", j=16)
                    link(nc.vector.tensor_copy(flat_hi[:, 16 * r:16 * r + 16, :], sf))
                    ins = nc.vector.tensor_tensor(flat_lo[:, 16 * r:16 * r + 16, :], sf, flat_hi[:, 16 * r:16 * r + 16, :].bitcast(f32), ALU.subtract)
                    if r == 1:
                        ins.then_inc(flat_done, 1)
                    else:
                        link(ins)

            def hidden(c):
                dve.wait_ge(hid_th, c + 1)
                f = hid[:, c, :, :].rearrange("p a m -> p (a m)")
                link(nc.vector.scalar_tensor_tensor(f, f, 1.0, ps[7][:, 0:64], ALU.add, ALU.mult))
                nc.vector.tensor_scalar(hid[:, c, :, :], hid[:, c, :, :], 0.5, None, ALU.mult).then_inc(hid_done, 1)

            def misc(m):
                if m == W2_K:
                    dve.wait_ge(m_pe, m + 1)
                    link(nc.vector.tensor_copy(kc[:].rearrange("p g d -> p (g d)"), log_ps[0:NCMP, 0:GROUPS * DH]))
                    for g in range(GROUPS):
                        link(nc.vector.tensor_tensor_reduce(sc[0][0:NCMP, 0, 0:DH], kc[:, g, :], kc[:, g, :], 1.0, 0.0, ALU.mult, ALU.add,
                                                            accum_out=scol["d"][0:NCMP, g:g + 1]))
                    link(nc.vector.tensor_scalar(scol["d"][0:NCMP, 2:4], scol["d"][0:NCMP, 0:2], 1.0 / DH, EPS, ALU.mult, ALU.add))
                    rsqrt(scol["d"][0:NCMP, 4:6], scol["d"][0:NCMP, 2:4], scol["d"][0:NCMP, 6:8])
                    nc.vector.tensor_tensor(kc[:], kc[:], scol["d"][0:NCMP, 4:6].unsqueeze(2).to_broadcast([NCMP, GROUPS, DH]), ALU.mult).then_inc(m_out, 1)
                elif m == LOGITS_C:
                    dve.wait_ge(m_pe, m + 1)
                    lg = log_ps[:, 0:HEADS * TT * 16].rearrange("p (h t n) -> p h t n", h=HEADS, t=TT)
                    link(nc.vector.memset(pc[:], NEG))
                    for t in range(TT):
                        k = NCMP if t else (P - CMP_BLOCK) // CMP_STRIDE + 1
                        first = P * (1 - t) + CMP_BLOCK - 1
                        link(nc.vector.tensor_tensor(pc[:, :, t, 0:k], lg[:, :, t, 0:k], col["rn"][:, :, t].unsqueeze(2).to_broadcast([P, HEADS, k]), ALU.mult))
                        link(nc.vector.tensor_tensor(pc[:, :, t, 0:k], pc[:, :, t, 0:k],
                                                     bias_g[:, :, first:first + CMP_STRIDE * (k - 1) + 1:CMP_STRIDE], ALU.add))
                    link(nc.vector.tensor_reduce(pcm[:].rearrange("p h t -> p (h t)"), pc[:].rearrange("p h t n -> p (h t) n"), AX.X, ALU.max))
                    nc.vector.tensor_tensor(pc[:].rearrange("p h t n -> p (h t) n"), pc[:].rearrange("p h t n -> p (h t) n"),
                                            pcm[:].rearrange("p h t -> p (h t)").unsqueeze(2).to_broadcast([P, 16, NCMP]), ALU.subtract).then_inc(pc_s, 1)
                    dve.wait_ge(pc_e, 1)
                    link(nc.vector.tensor_reduce(pcs[:].rearrange("p h t -> p (h t)"), pc[:].rearrange("p h t n -> p (h t) n"), AX.X, ALU.add))
                    link(nc.vector.reciprocal(pcs[:], pcs[:]))
                    link(nc.vector.tensor_scalar(pcs[:, :, 0], pcs[:, :, 0], rowvalid[:], None, ALU.mult))
                    g0 = gates[:].rearrange("p t (h b) -> p h t b", b=3)[:, :, :, 0]
                    link(nc.vector.tensor_tensor(pcs[:], pcs[:], g0, ALU.mult))
                    nc.vector.tensor_tensor(pc[:].rearrange("p h t n -> p (h t) n"), pc[:].rearrange("p h t n -> p (h t) n"),
                                            pcs[:].rearrange("p h t -> p (h t)").unsqueeze(2).to_broadcast([P, 16, NCMP]), ALU.mult).then_inc(m_out, 1)

            def unit(i):
                if i < len(UNITS):
                    h, t = UNITS[i]
                    w = P * (t + 1)
                    dve.wait_ge(l_mm, i + 1)
                    if i >= 3:
                        dve.wait_ge(t_mm, i - 2)
                    s = sc[i % 3][:, :, 0:w]
                    lg = log_ps[:].rearrange("p (a c) -> p a c", a=2)[:, :, 0:w]
                    bg = bias_g[:, h, SEQ - w:SEQ].unsqueeze(1).to_broadcast([P, 2, w])
                    link(nc.vector.scalar_tensor_tensor(s, lg, col["rn"][:, h, t:t + 1], bg, ALU.mult, ALU.add))
                    nc.vector.tensor_reduce(scol["nm"][:, 2 * (i % 3):2 * (i % 3) + 2], s, AX.X, ALU.max, negate=True).then_inc(s_done, 1)
                if 1 <= i <= len(UNITS):
                    j = i - 1
                    h, t = UNITS[j]
                    w = P * (t + 1)
                    dve.wait_ge(e_done, 2 * j + 2)
                    c2 = slice(2 * (j % 3), 2 * (j % 3) + 2)
                    link(nc.vector.reciprocal(scol["fac"][:, c2], scol["se"][:, c2]))
                    link(nc.vector.tensor_tensor(scol["fac"][:, c2], scol["fac"][:, c2], gates[:, t, 3 * h + 1:3 * h + 3], ALU.mult))
                    for a in range(2):
                        nc.vector.tensor_scalar(sc[j % 3][:, a, 0:w], sc[j % 3][:, a, 0:w], scol["fac"][:, 2 * (j % 3) + a:2 * (j % 3) + a + 1],
                                                None, ALU.mult).then_inc(p_done, 1)

            def evacuate(n):
                kind, i = CHUNKS[n]
                if n not in BANK_USE:
                    return
                u = BANK_USE[n]
                bank = stream_ps[u % 2][:].rearrange("p (a c) -> p a c", a=2)
                if kind == "gz":
                    dve.wait_ge(zt, i + 1)
                    nc.vector.scalar_tensor_tensor(zsT[:, 2 * i:2 * i + 2, :], gate_t[:], 1.0, bank, ALU.add, ALU.mult).then_inc(zs_done, 1)
                elif kind == "pa":
                    dve.wait_ge(mg_done, i + 1)
                    dve.wait_ge(half_done, 2 * n + 2)
                    nc.vector.scalar_tensor_tensor(mix[:, 2 * i:2 * i + 2, :], gates_t[i % 2][:], 1.0, bank, ALU.add, ALU.mult).then_inc(pa_done, 1)
                elif kind == "pb":
                    dve.wait_ge(mg_done, 4 + i + 1)
                    dve.wait_ge(half_done, 2 * n + 2)
                    nc.vector.scalar_tensor_tensor(pmix[:], gates_t[i % 2][:], 1.0, bank, ALU.add, ALU.mult).then_inc(pb_read, 1)
                elif kind == "wo":
                    dve.wait_ge(half_done, 2 * n + 2)
                    dve.wait_ge(xres_in, 16)
                    nc.vector.tensor_tensor(x1[:, :, i * CW:(i + 1) * CW], x1[:, :, i * CW:(i + 1) * CW], bank, ALU.add).then_inc(x1_done, 1)
                elif kind == "gu":
                    dve.wait_ge(sg_done, i + 1)
                    if i >= 2:
                        dve.wait_ge(g_hi_done, i - 1)
                    nc.vector.tensor_tensor(gu[i % 2][:], sg[i % 2][:], bank[:, 1, :], ALU.mult).then_inc(gu_done, 1)

            def evacuate_late(n):
                kind, i = CHUNKS[n]
                if kind == "pb":
                    dve.wait_ge(pb_read, i + 1)
                    nc.vector.tensor_tensor(mix[:, 2 * i:2 * i + 2, :], mix[:, 2 * i:2 * i + 2, :], pmix[:], ALU.add).then_inc(mix_done, 1)
                    dve.wait_ge(mix_hi_done, i + 1)
                    nc.vector.scalar_tensor_tensor(mix_lo[:, 2 * i:2 * i + 2, :], mix[:, 2 * i:2 * i + 2, :], 0.5,
                                                   mix_hi[:, 2 * i:2 * i + 2, :].bitcast(f32), ALU.mult, ALU.subtract).then_inc(mix_lo_done, 1)
                elif kind == "gu":
                    dve.wait_ge(g_hi_done, i + 1)
                    nc.vector.tensor_tensor(g_lo[i % 4][:], gu[i % 2][:], g_hi[i % 4][:].bitcast(f32), ALU.subtract).then_inc(g_lo_done, 1)

            for n in range(len(CHUNKS) + 1):
                kind, _ = CHUNKS[n] if n < len(CHUNKS) else (None, 0)
                if n == 0:
                    split_lo(1)
                    small_gates()
                else:
                    if n > FIRST_STAGE_SLOT:
                        evacuate(n - 1)
                    if CHUNKS[n - 1] in LAST_OF_KIND:
                        evacuate_late(n - 1)
                    if n == AT["gu", 0]:
                        dve.wait_ge(xss, TT + 4 * TT)
                        link(nc.vector.tensor_reduce(scol["x"][:, 0:2], xs[:], AX.X, ALU.add))
                        normalise(x1, x1n, 4 * TT)
                        h_low(KT, ROW_N2)
                    if n + 1 < len(CHUNKS):
                        split_lo(n + 1)
                    if CHUNKS[n - 1] not in LAST_OF_KIND:
                        evacuate_late(n - 1)
                if 2 <= n <= FIRST_STAGE_SLOT:
                    conv_finish(n - 2)
                if 1 <= n < FIRST_STAGE_SLOT:
                    conv(n - 1)
                if n == 1:
                    decay_factors()
                if n == AT["mga", 1]:
                    for b in range(NB):
                        dve.wait_ge(ya_hi_done, b + 1)
                        nc.vector.tensor_tensor(ya_lo[:, 2 * b:2 * b + 2, :], zsT[:, 2 * b:2 * b + 2, :], ya_hi[:, 2 * b:2 * b + 2, :].bitcast(f32), ALU.subtract).then_inc(ya_lo_done, 1)
                if n == 2:
                    for i in range(4):
                        dve.wait_ge(bias_mm, i + 1)
                        nc.vector.tensor_copy(bias_g[:, 2 * i:2 * i + 2, :].rearrange("p h c -> p (h c)"), flip_ps[i][:]).then_inc(bias_done, 1)
                if n == 7:
                    dve.wait_ge(colsum, 4)
                    inverse_norm("rk", ps[5], 0.25, EPS, 0.5).then_inc(rk_ready, 1)
                    dve.wait_ge(rk_ready, 1)
                if n == 11:
                    dve.wait_ge(colsum, 8)
                    inverse_norm("rq", ps[6], 0.25, EPS, 0.5 * DH ** -0.5).then_inc(rq_ready, 1)
                    dve.wait_ge(rq_ready, 1)
                for half in range(2):
                    for name in slot_stages(n, half):
                        gdn(name)
                    if (n, half) == (FIRST_STAGE_SLOT, 0):
                        conv(n - 1)
                        conv_finish(n - 1)
                    if half == 1 and n - 1 in (AT["cmpk", 3], AT["cmpv", 3]):
                        hidden(0 if n - 1 == AT["cmpk", 3] else 1)
                    if half == 0:
                        if n == AT["cmpv", 0]:
                            dve.wait_ge(colsum, 12)
                            inverse_norm("rn", ps[7], 1.0 / DH, EPS, 1.0).then_inc(rn_ready, 1)
                            dve.wait_ge(rn_ready, 1)
                        if n == AT["ks", 0] + 1:
                            keys(0)
                        if n == AT["kw", 0] + 1:
                            keys(1)
                        if n == AT["kc", 0] + 1:
                            flatten(0)
                        if n == AT["cmpk", 3] + 1:
                            flatten(1)
                    for m in slot_misc(n, half):
                        misc(m)
                    for i in slot_units(n, half):
                        unit(i)
                if n == AT["mgb", 0]:
                    for b in range(NB):
                        dve.wait_ge(yb_hi_done, b + 1)
                        nc.vector.tensor_tensor(yb_lo[:, 2 * b:2 * b + 2, :], nqT[:, 2 * b:2 * b + 2, :], yb_hi[:, 2 * b:2 * b + 2, :].bitcast(f32), ALU.subtract).then_inc(yb_lo_done, 1)
            for i in range(4):
                dve.wait_ge(half_done, 2 * len(CHUNKS))
                t, c = i // 2, i % 2
                nc.vector.tensor_tensor(out_sb[:, t, c * 512:(c + 1) * 512], x1[:, t, c * 512:(c + 1) * 512], ps[4 + i][:], ALU.add).then_inc(fin, 1)

        @block.tensor
        def _(pe):
            def three(pairs, bank, lhs, rhs, start, stop):
                (lh, ll), (rh, rl) = pairs
                pe.matmul(bank, lhs(lh), rhs(rh), start=start, stop=False)
                pe.matmul(bank, lhs(lh), rhs(rl), start=False, stop=False)
                return pe.matmul(bank, lhs(ll), rhs(rh), start=False, stop=stop)

            def transpose(o, i, n=P):
                return pe.transpose(o, i, ident[0:n, 0:n])

            def to_channels(src, before):
                pe.wait_ge(xn_done, before)
                for k in range(KT):
                    for t in range(TT):
                        o = (k % 2) * SEQ + t * P
                        last = transpose(ps[2 + k // 2][:, o:o + P], src[:, t, k * P:(k + 1) * P])
                    if k % 2:
                        last.then_inc(tr_ready, 1)

            pe.wait_ge(ident_in, 16)
            pe.wait_ge(vec_in, 112)
            transpose(ps[7][:, 0:CONV * 24], rows_a[:], CONV * 24).then_inc(pre_pe, 1)
            transpose(ps[7][:, P:P + NROWS], rows_b[:], NROWS).then_inc(pre_pe, 1)
            to_channels(xn_sb, TT)
            pe.wait_ge(misc_in, 96)
            pe.matmul(ps[6][0:HEADS, 0:384], relb[:], onehot[:], start=True, stop=True).then_inc(pre_pe, 1)
            pe.wait_ge(pre_act, 1)
            pe.wait_ge(pre_dve, 3)
            for k in range(KT):
                pe.wait_ge(h_hi_done, k + 1)
                pe.wait_ge(h_lo_done, k + 1)
                last = three(((wsm_hi, wsm_lo), (h_hi, h_lo)), ps[1][0:NSMALL, 0:SEQ],
                             lambda a: a[:, k, :], lambda a: a[:, k, :], k == 0, k == KT - 1)
            last.then_inc(pre_pe, 1)

            def decay_columns():
                pe.wait_ge(const_in, 32)
                pe.wait_ge(pre_dve, 5)
                pe.wait_ge(ones_set, 2)
                for t in range(TT):
                    pe.matmul(ps[7][:, 384 + t:400:2], upper[:], col["g"][:, :, t], start=True, stop=True)
                    last = pe.matmul(ps[7][:, 400 + t:416:2], ones_sq[:], col["g"][:, :, t], start=True, stop=True)
                last.then_inc(pre_pe, 1)

            def half_chunk(n, half):
                kind, i = CHUNKS[n]
                hi, lo = w_hi[n % NSPL], w_lo[n % NSPL]
                if half == 0:
                    pe.wait_ge(hi_done, n + 1)
                    pe.wait_ge(lo_done, n + 1)
                    wait_bank(pe, n)
                acts, split = (h_hi, h_lo), None
                if kind == "pa":
                    acts, split = (ya_hi, ya_lo), (ya_hi_done, ya_lo_done)
                if kind == "pb":
                    acts, split = (yb_hi, yb_lo), (yb_hi_done, yb_lo_done)
                if kind == "wo":
                    acts, split = (mix_hi, mix_lo), (mix_hi_done, mix_lo_done)
                if n == AT["gu", 0] and half == 0:
                    to_channels(x1n, 2 * TT)
                if kind in ("cmpk", "cmpv"):
                    c = 0 if kind == "cmpk" else 1
                    if i == 0 and half == 0:
                        pe.wait_ge(flat_done, c + 1)
                        if c == 1:
                            pe.wait_ge(hid_raw, 1)
                        else:
                            pe.wait_ge(rq_ready, 1)
                    for j in range(half * KT // 2, (half + 1) * KT // 2):
                        last = three(((flat_hi, flat_lo), (hi, lo)), ps[6][0:32, 0:CW], lambda a: a[:, i * KT + j, :],
                                     lambda a: a[:, j, :], i == 0 and j == 0, i == 3 and j == KT - 1)
                elif kind == "dn":
                    h2, l2 = (w[:].rearrange("p k c -> p (k c)").rearrange("p (k c) -> p k c", k=2) for w in (hi, lo))
                    tile_no = 2 * i + half
                    pe.wait_ge(g_hi_done, tile_no + 1)
                    pe.wait_ge(g_lo_done, tile_no + 1)
                    gh, gl = g_hi[tile_no % 4], g_lo[tile_no % 4]
                    for t in range(TT):
                        for c in range(2):
                            last = three(((gh, gl), (h2, l2)), ps[4 + 2 * t + c][:],
                                         lambda a: a[:, t * P:(t + 1) * P], lambda a: a[:, half, c * 512:(c + 1) * 512],
                                         tile_no == 0, tile_no == FFN // P - 1)
                else:
                    bank = stream_ps[BANK_USE[n] % 2][:, half * SEQ:(half + 1) * SEQ]
                    for k in range(KT):
                        if n == AT["gu", 0] and half == 0:
                            pe.wait_ge(h_hi_done, KT + k + 1)
                            pe.wait_ge(h_lo_done, KT + k + 1)
                        if split and i == 0 and half == 0 and k % 2 == 0:
                            for parts in split:
                                pe.wait_ge(parts, k // 2 + 1)
                        if kind in TOKEN_MAJOR:
                            last = three((acts, (hi, lo)), bank, lambda a: a[:, k, half * P:(half + 1) * P], lambda a: a[:, k, :],
                                         k == 0, k == KT - 1)
                        else:
                            last = three(((hi, lo), acts), bank, lambda a: a[:, k, half * P:(half + 1) * P], lambda a: a[:, k, :],
                                         k == 0, k == KT - 1)
                return last

            def column_sums(sq, bank, first, is_ready, value):
                pe.wait_ge(is_ready, value)
                for a in range(2):
                    for t in range(TT):
                        last = pe.matmul(bank[:, first + 2 * a + t:first + 2 * a + t + 1], sq[:, a, t * P:(t + 1) * P], ones[:, 0:1],
                                         start=True, stop=True)
                last.then_inc(colsum, 1)

            def gdn(name):
                for b in range(NB):
                    u = stage_use(name, b)
                    if name == "ot" and b == GRING:
                        pe.wait_ge(zs_done, 4 + 1)
                    elif u >= GRING:
                        pe.wait_ge(g_out[u % GRING], u // GRING)
                    b4 = gdn_ps[u % GRING][:].rearrange("p (q c) -> p q c", q=4)
                    p4 = lambda t: problems(t, b)
                    mm = lambda q, lhsT, rhs, start=True, stop=True: pe.matmul(b4[:, q, :], lhsT, rhs, start=start, stop=stop)
                    if name == "row":
                        pe.wait_ge(pre_dve, 5)
                        if b == 0:
                            pe.wait_ge(rk_ready, 1)
                        for q in range(4):
                            last = mm(q, pcol("g", b)[:, q:q + 1].to_broadcast([P, P]), upper[:])
                    elif name in ("kt", "vt"):
                        pe.wait_ge(conv_done, b + 1 + (8 if name == "vt" else 0))
                        for q in range(4):
                            last = transpose(b4[:, q, :], p4(kT if name == "kt" else vT)[:, q, :])
                    elif name in ("knT", "m1t", "at", "ot"):
                        src, before = {"knT": (kn, "kt"), "m1t": (AXb, "gram"), "at": (AXb, "m1t"), "ot": (kT, None)}[name]
                        if before:
                            wait_use(pe, before, b)
                        else:
                            pe.wait_ge(on_ready, b + 1)
                        for q in range(4):
                            last = transpose(b4[:, q, :], p4(src)[:, q, :])
                    elif name in ("gram", "kq"):
                        wait_use(pe, "knT", b)
                        for q in range(4):
                            last = mm(q, p4(kT)[:, q, :], p4(kT if name == "gram" else qT)[:, q, :])
                    elif name[0] == "X":
                        l = int(name[1:])
                        if l == 1:
                            pe.wait_ge(lvl0, b + 1)
                        else:
                            wait_use(pe, f"Y{l - 1}", b)
                        c = level_columns(name)
                        for q in range(4):
                            last = pe.matmul(b4[:, q, c], p4(ATb)[:, q, :], p4(Db)[:, q, c], start=True, stop=True)
                    elif name[0] in "YZ":
                        l = int(name[1:])
                        wait_use(pe, f"X{l}", b)
                        if l > 1:
                            wait_use(pe, f"Z{l - 1}", b)
                        for q in range(4):
                            if name[0] == "Y":
                                last = mm(q, p4(DTb)[:, q, :], p4(AXb)[:, q, :])
                            else:
                                c = level_columns(name)
                                last = pe.matmul(b4[:, q, c], p4(AXb)[:, q, :], p4(DTb)[:, q, c], start=True, stop=True)
                    elif name == "w0":
                        wait_use(pe, f"Z{LEVELS - 1}", b)
                        wait_use(pe, "vt", b)
                        pe.wait_ge(kf_ready, b + 1)
                        for hh in range(2):
                            mm(hh, p4(DTb)[:, 2 * hh, :], p4(vT)[:, 2 * hh, :])
                        for hh in range(2):
                            last = mm(2 + hh, p4(kn)[:, 2 * hh + 1, :], p4(DTb)[:, 2 * hh + 1, :])
                    elif name == "s1":
                        wait_use(pe, "w0", b)
                        wait_use(pe, "kq", b)
                        for hh in range(2):
                            mm(hh, p4(kn)[:, 2 * hh, :], p4(AXb)[:, 2 * hh, :])
                        for hh in range(2):
                            last = mm(2 + hh, p4(ET)[:, 2 * hh, :], p4(AXb)[:, 2 * hh, :])
                    elif name == "v1":
                        wait_use(pe, "s1", b)
                        for hh in range(2):
                            mm(hh, p4(DTb)[:, 2 * hh + 1, :], p4(vT)[:, 2 * hh + 1, :], True, False)
                            mm(hh, p4(Db)[:, 2 * hh + 1, :], p4(Db)[:, 2 * hh, :], False, True)
                        for hh in range(2):
                            last = mm(2 + hh, p4(qT)[:, 2 * hh + 1, :], p4(Db)[:, 2 * hh, :])
                    elif name == "o1":
                        wait_use(pe, "v1", b)
                        for hh in range(2):
                            last = mm(hh, p4(ET)[:, 2 * hh + 1, :], p4(AXb)[:, 2 * hh + 1, :])
                    last.then_inc(g_mm, 1)

            def misc(m):
                if m >= 1:
                    pe.wait_ge(m_out, m)
                if m in (TURN_KS, TURN_KW):
                    j = m - TURN_KS
                    pe.wait_ge(key_n, j + 1)
                    for q in range(4):
                        last = transpose(log_ps[:, q * P:(q + 1) * P], key_tok[:, j, q, :])
                elif m in (W2_K, W2_V):
                    c = 0 if m == W2_K else 1
                    pe.wait_ge(hid_done, c + 1)
                    if c == 0:
                        pe.wait_ge(rk_ready, 1)
                    for g in range(GROUPS):
                        for a in range(2):
                            last = pe.matmul(log_ps[0:NCMP, g * DH:(g + 1) * DH], hid[:, c, a, g * 16:g * 16 + NCMP], cmp2[:, c, a, :],
                                             start=(a == 0), stop=(a == 1))
                elif m == TURN_KC:
                    for g in range(GROUPS):
                        last = transpose(log_ps[:, g * 16:g * 16 + NCMP], kc[:, g, :], NCMP)
                elif m == LOGITS_C:
                    pe.wait_ge(copied, COPY_NO[AT["nq", 3]] + 1)
                    for h in range(HEADS):
                        for t in range(TT):
                            o = (h * TT + t) * 16
                            last = pe.matmul(log_ps[:, o:o + NCMP], nqT[:, h, t * P:(t + 1) * P], kcT[:, h // 4, 0:NCMP], start=True, stop=True)
                else:
                    for q in range(4):
                        h, t = UNITS[4 * (m - TURN_PC) + q]
                        last = transpose(log_ps[0:NCMP, q * P:(q + 1) * P], pc[:, h, t, :])
                last.then_inc(m_pe, 1)

            def unit(i):
                if i < len(UNITS):
                    h, t = UNITS[i]
                    w = P * (t + 1)
                    if i >= 1:
                        pe.wait_ge(s_done, i)
                    else:
                        pe.wait_ge(m_out, 10)
                    for a, keys in enumerate((ksT, kwT)):
                        last = pe.matmul(log_ps[:, a * SEQ:a * SEQ + w], nqT[:, h, t * P:(t + 1) * P], keys[:, h // 4, 0:w], start=True, stop=True)
                    last.then_inc(l_mm, 1)
                if 2 <= i < len(UNITS) + 2:
                    j = i - 2
                    h, t = UNITS[j]
                    pe.wait_ge(p_done, 2 * j + 2)
                    if j >= 1:
                        pe.wait_ge(t_out, j)
                    for a in range(2):
                        for k in range(t + 1):
                            o = (a * (t + 1) + k) * P
                            last = transpose(pt_ps[:, o:o + P], sc[j % 3][:, a, k * P:(k + 1) * P])
                    last.then_inc(t_mm, 1)
                if i >= 3:
                    j = i - 3
                    h, t = UNITS[j]
                    g = h // 4
                    pe.wait_ge(t_out, j + 1)
                    if j >= 1:
                        pe.wait_ge(v_out, j)
                    o = pv_ps[:, 0:P]
                    kk = NCMP if t else (P - CMP_BLOCK) // CMP_STRIDE + 1
                    pe.matmul(o, vc[0:kk, g, :], pcT[0:kk, j, :], start=True, stop=False)
                    for a, values in enumerate((vs, vw)):
                        for k in range(t + 1):
                            last = pe.matmul(o, values[:, k, g, :], pt[j % 2][:, a * (t + 1) + k, :], start=False, stop=(a == 1 and k == t))
                    last.then_inc(v_mm, 1)

            for n in range(len(CHUNKS)):
                kind, _ = CHUNKS[n]
                for half in range(2):
                    last = half_chunk(n, half)
                    last.then_inc(half_done, 1)
                    if n == 0 and half == 0:
                        pe.wait_ge(small_raw, 1)
                        for t in range(TT):
                            last = transpose(ps[7][:, 256 + t * NSMALL:256 + (t + 1) * NSMALL], small_ch[:, t * P:(t + 1) * P], NSMALL)
                        last.then_inc(small_mm, 1)
                    if n == 1 and half == 1:
                        decay_columns()
                        pe.wait_ge(bias_in, 32)
                        for i in range(4):
                            pe.matmul(flip_ps[i][:], flip[:], bias_up[:, 2 * i:2 * i + 2, :].rearrange("p h c -> p (h c)"),
                                      start=True, stop=True).then_inc(bias_mm, 1)
                    if 3 <= n <= 10 and half == 0:
                        k = n - 3
                        if k == 4:
                            pe.wait_ge(bias_done, 4)
                        column_sums(csq[k % 2], ps[5] if k < 4 else ps[6], 4 * (k % 4), conv_sq, k + 1)
                    if AT["nq", 0] + 1 <= n <= AT["nq", 3] + 1 and half == 1:
                        k = n - AT["nq", 0] - 1
                        if k == 0:
                            pe.wait_ge(hid_done, 1)
                        column_sums(nsq, ps[7], 4 * k, nq_sq, k + 1)
                    if half == 0 and n - 1 in (AT["cmpk", 3], AT["cmpv", 3]):
                        c = 0 if n - 1 == AT["cmpk", 3] else 1
                        if c == 1:
                            pe.wait_ge(rn_ready, 1)
                        pe.wait_ge(hid_raw, c + 1)
                        for a in range(2):
                            last = transpose(ps[7][:, a * 32:(a + 1) * 32], hid_tok[:, a * P:(a + 1) * P], 32)
                        last.then_inc(hid_mm, 1)
                    for name in slot_stages(n, half):
                        gdn(name)
                    for m in slot_misc(n, half):
                        misc(m)
                    for i in slot_units(n, half):
                        unit(i)


def shape_constants():
    i = np.arange(P)
    ident = np.eye(P, dtype=np.float32)
    upper = (i[:, None] <= i[None, :]).astype(np.float32)
    negmask = np.where(i[:, None] <= i[None, :], 0.0, NEG).astype(np.float32)
    levels = np.zeros((P, 2 * LEVELS, P), np.float32)
    for l in range(LEVELS):
        s = 1 << l
        m = (i[:, None] // (2 * s) == i[None, :] // (2 * s)) & (i[:, None] // s % 2 == 1) & (i[None, :] // s % 2 == 0)
        levels[:, l, :] = m
        levels[:, LEVELS + l, :] = m.T
    dist = SEQ - 1 - np.arange(384)
    d = np.maximum(dist, 0)
    exact = REL_BUCKETS // 2
    large = exact + (np.log(np.maximum(d, 1).astype(np.float32) / np.float32(exact)) / np.float32(math.log(REL_MAX_DIST / exact))
                     * np.float32(REL_BUCKETS - exact)).astype(np.int32)
    bucket = np.where(d < exact, d, np.minimum(large, REL_BUCKETS - 1))
    onehot = np.zeros((REL_BUCKETS + 1, 384), np.float32)
    onehot[bucket, np.arange(384)] = 1.0
    onehot[REL_BUCKETS, dist < 0] = NEG
    rowvalid = (i >= CMP_BLOCK - 1).astype(np.float32)[:, None]
    return {"c_ident": ident, "c_upper": upper, "c_negmask": negmask, "c_levels": levels, "c_onehot": onehot, "c_rowvalid": rowvalid,
            "c_flip": np.ascontiguousarray(ident[::-1])}


INS = ["x", "norm1_w", "w_in", "conv_w", "a_log", "dt_bias", "gdn_norm_w", "cmp_pe", "cmp_w1", "cmp_w2", "q_norm_w", "k_norm_w",
       "rel_bias", "w_proj_a", "w_proj_b", "w_out", "norm2_w", "w_gate", "w_up", "w_down"]


def kernel(**inputs):
    import concourse.bacc as bacc
    from concourse.bass_utils import run_bass_kernel_spmd

    nc = bacc.Bacc("TRN2", target_bir_lowering=False, num_devices=1)
    arrays = {n: np.ascontiguousarray(inputs[n]) for n in INS}
    arrays.update(shape_constants())
    args = [nc.dram_tensor("in_" + n, a.shape, mybir.dt.from_np(a.dtype), kind="ExternalInput").ap() for n, a in arrays.items()]
    scratch = nc.dram_tensor("bias_rows", [HEADS, 384], mybir.dt.float32, kind="Internal").ap()
    out = nc.dram_tensor("out_0", [1, SEQ, D_MODEL], mybir.dt.float32, kind="ExternalOutput").ap()
    hybrid_block(nc, *args, scratch, out)
    r = run_bass_kernel_spmd(nc, [{"in_" + n: a for n, a in arrays.items()}], core_ids=[0])
    return r.results[0]["out_0"]
```
